# Optimizing a Trainium2 kernel written in Bass

```python
import math
import jax
import jax.numpy as jnp
from jax import lax
import numpy as np

"""Hybrid decoder block with two parallel causal token mixers merged by learned sigmoid gates.

One layer: h = x + W_out( sigmoid(g_ret) * (o_ret @ W_ret_up) + sigmoid(g_diff) * (o_diff @ W_diff_up) ),
where o_ret is multi-scale retention in chunkwise-recurrent form (RetNet) and o_diff is
differential attention (Diff-Transformer) with rotary positions. Each branch output is
multiplied by a SiLU gate path of its own width. All q/k/v, SiLU gate paths and merge gates
come from ONE combined input projection of the RMS-normalised input. Output = final RMSNorm.

Inputs: x (BATCH, SEQ, D_MODEL) float32 plus weights. Output: (BATCH, SEQ, D_MODEL).
"""

D_MODEL = 2048
BATCH = 1
SEQ = 256
DEPTH = 1

RET_QK_DIM = 128
RET_V_DIM = 256
RET_HEADS = D_MODEL // RET_V_DIM
RET_QK_WIDTH = RET_HEADS * RET_QK_DIM
RET_WIDTH = RET_HEADS * RET_V_DIM
CHUNK = 128

DIFF_HEAD_DIM = 128
DIFF_V_DIM = 2 * DIFF_HEAD_DIM
DIFF_HEADS = D_MODEL // DIFF_V_DIM
DIFF_QK_WIDTH = DIFF_HEADS * 2 * DIFF_HEAD_DIM
DIFF_WIDTH = DIFF_HEADS * DIFF_V_DIM
Q_BLOCK = 128
ROPE_THETA = 10000.0

NORM_EPS = 1e-6
SUBLN_EPS = 1e-5

SPLIT_SIZES = (RET_QK_WIDTH, RET_QK_WIDTH, RET_WIDTH, RET_WIDTH,
               DIFF_QK_WIDTH, DIFF_QK_WIDTH, DIFF_WIDTH, DIFF_WIDTH,
               D_MODEL, D_MODEL)
SPLIT_POINTS = tuple(int(v) for v in np.cumsum(SPLIT_SIZES)[:-1])
IN_WIDTH = int(sum(SPLIT_SIZES))

kernel_name = 'hybrid_retention_diffattn_gated_block'

def rmsnorm(x, w, eps):
    xf = x.astype(jnp.float32)
    y = xf * lax.rsqrt(jnp.mean(xf * xf, axis=-1, keepdims=True) + eps)
    if w is not None:
        y = y * w.astype(jnp.float32)
    return y.astype(x.dtype)

def rotary_tables(pos, inv_freq, dtype):
    ang = pos[:, None] * inv_freq[None, :]
    emb = jnp.concatenate([ang, ang], axis=-1)
    return jnp.cos(emb).astype(dtype)[:, None, :], jnp.sin(emb).astype(dtype)[:, None, :]

def rotate_half(x):
    x1, x2 = jnp.split(x, 2, axis=-1)
    return jnp.concatenate([-x2, x1], axis=-1)

def apply_rotary(x, cos, sin):
    return x * cos + rotate_half(x) * sin

def retention(q, k, v):
    b, s, h, dk = q.shape
    dv = v.shape[-1]
    n = s // CHUNK
    log_gamma = jnp.log1p(-jnp.exp2(-5.0 - jnp.arange(h, dtype=jnp.float32)))
    qc = q.reshape(b, n, CHUNK, h, dk)
    kc = k.reshape(b, n, CHUNK, h, dk)
    vc = v.reshape(b, n, CHUNK, h, dv)
    idx = jnp.arange(CHUNK, dtype=jnp.float32)
    rel = idx[:, None] - idx[None, :]
    decay_mask = jnp.where(rel >= 0.0,
                           jnp.exp(log_gamma[:, None, None] * jnp.maximum(rel, 0.0)[None]),
                           0.0)
    scores = jnp.einsum('bnqhd,bnkhd->bnhqk', qc, kc) * decay_mask
    o_intra = jnp.einsum('bnhqk,bnkhe->bnqhe', scores, vc)
    zeta = jnp.exp(log_gamma[None, :] * (CHUNK - 1.0 - idx)[:, None])
    kv = jnp.einsum('bnkhd,bnkhe->bnhde', kc, vc * zeta[:, :, None])
    chunk_decay = jnp.exp(log_gamma * CHUNK)[:, None, None]

    def step(state, kv_i):
        return state * chunk_decay + kv_i, state

    init = jnp.zeros((b, h, dk, dv), kv.dtype)
    _, prev = lax.scan(step, init, jnp.moveaxis(kv, 1, 0))
    prev = jnp.moveaxis(prev, 0, 1)
    xi = jnp.exp(log_gamma[None, :] * (idx + 1.0)[:, None])
    o_cross = jnp.einsum('bnqhd,bnhde->bnqhe', qc, prev) * xi[:, :, None]
    return (o_intra + o_cross).reshape(b, s, h, dv)

def diff_attention(q, k, v, lam):
    b, s, h, _, d = q.shape
    n = s // Q_BLOCK
    qb = (q * (d ** -0.5)).reshape(b, n, Q_BLOCK, h, 2, d)
    qb = jnp.moveaxis(qb, 1, 0)
    key_pos = jnp.arange(s)

    def block(args):
        q_blk, i = args
        q_pos = i * Q_BLOCK + jnp.arange(Q_BLOCK)
        scores = jnp.einsum('bqhcd,bkhcd->bhcqk', q_blk, k).astype(jnp.float32)
        causal = key_pos[None, :] <= q_pos[:, None]
        scores = jnp.where(causal, scores, -jnp.inf)
        probs = jax.nn.softmax(scores, axis=-1)
        attn = probs[:, :, 0] - lam * probs[:, :, 1]
        return jnp.einsum('bhqk,bkhe->bqhe', attn.astype(v.dtype), v)

    out = lax.map(block, (qb, jnp.arange(n)))
    return jnp.moveaxis(out, 0, 1).reshape(b, s, h, 2 * d)

def setup_inputs(seed: int = 0) -> dict:
    key = jax.random.key(seed)
    ks = jax.random.split(key, 12)
    f32 = jnp.float32
    x = jax.random.normal(ks[0], (BATCH, SEQ, D_MODEL), f32)
    norm_w = 1.0 + 0.02 * jax.random.normal(ks[1], (DEPTH, D_MODEL), f32)
    w_in = jax.random.normal(ks[2], (DEPTH, D_MODEL, IN_WIDTH), f32) * D_MODEL ** -0.5
    w_ret_up = jax.random.normal(ks[3], (DEPTH, RET_WIDTH, D_MODEL), f32) * RET_WIDTH ** -0.5
    w_diff_up = jax.random.normal(ks[4], (DEPTH, DIFF_WIDTH, D_MODEL), f32) * DIFF_WIDTH ** -0.5
    w_out = jax.random.normal(ks[5], (DEPTH, D_MODEL, D_MODEL), f32) * D_MODEL ** -0.5
    lambda_q1 = 0.1 * jax.random.normal(ks[6], (DEPTH, DIFF_HEAD_DIM), f32)
    lambda_k1 = 0.1 * jax.random.normal(ks[7], (DEPTH, DIFF_HEAD_DIM), f32)
    lambda_q2 = 0.1 * jax.random.normal(ks[8], (DEPTH, DIFF_HEAD_DIM), f32)
    lambda_k2 = 0.1 * jax.random.normal(ks[9], (DEPTH, DIFF_HEAD_DIM), f32)
    subln_w = 1.0 + 0.02 * jax.random.normal(ks[10], (DEPTH, DIFF_V_DIM), f32)
    final_norm_w = 1.0 + 0.02 * jax.random.normal(ks[11], (D_MODEL,), f32)
    return {'x': x, 'norm_w': norm_w, 'w_in': w_in, 'w_ret_up': w_ret_up,
            'w_diff_up': w_diff_up, 'w_out': w_out, 'lambda_q1': lambda_q1,
            'lambda_k1': lambda_k1, 'lambda_q2': lambda_q2, 'lambda_k2': lambda_k2,
            'subln_w': subln_w, 'final_norm_w': final_norm_w}

def reference(x, norm_w, w_in, w_ret_up, w_diff_up, w_out, lambda_q1, lambda_k1,
              lambda_q2, lambda_k2, subln_w, final_norm_w):
    b, s, _ = x.shape
    pos = jnp.arange(s, dtype=jnp.float32)
    ret_inv_freq = jnp.exp(-math.log(10000.0) * jnp.linspace(0.0, 1.0, RET_QK_DIM // 2, dtype=jnp.float32))
    rope_inv_freq = ROPE_THETA ** (-jnp.arange(0, DIFF_HEAD_DIM, 2, dtype=jnp.float32) / DIFF_HEAD_DIM)
    ret_cos, ret_sin = rotary_tables(pos, ret_inv_freq, x.dtype)
    rope_cos, rope_sin = rotary_tables(pos, rope_inv_freq, x.dtype)

    h = x
    for l in range(DEPTH):
        xn = rmsnorm(h, norm_w[l], NORM_EPS)
        proj = xn @ w_in[l]
        (rq, rk, rv, rz, dq, dk, dv, dz, g_ret, g_diff) = jnp.split(proj, SPLIT_POINTS, axis=-1)

        rq = apply_rotary(rq.reshape(b, s, RET_HEADS, RET_QK_DIM), ret_cos, ret_sin)
        rk = apply_rotary(rk.reshape(b, s, RET_HEADS, RET_QK_DIM) * (RET_QK_DIM ** -0.5), ret_cos, ret_sin)
        rv = rv.reshape(b, s, RET_HEADS, RET_V_DIM)
        o_ret = retention(rq, rk, rv).astype(h.dtype)
        o_ret = rmsnorm(o_ret, None, NORM_EPS).reshape(b, s, RET_WIDTH)
        o_ret = o_ret * jax.nn.silu(rz)

        dq = apply_rotary(dq.reshape(b, s, 2 * DIFF_HEADS, DIFF_HEAD_DIM), rope_cos, rope_sin)
        dk = apply_rotary(dk.reshape(b, s, 2 * DIFF_HEADS, DIFF_HEAD_DIM), rope_cos, rope_sin)
        dq = dq.reshape(b, s, DIFF_HEADS, 2, DIFF_HEAD_DIM)
        dk = dk.reshape(b, s, DIFF_HEADS, 2, DIFF_HEAD_DIM)
        dv = dv.reshape(b, s, DIFF_HEADS, DIFF_V_DIM)
        lam_init = 0.8 - 0.6 * math.exp(-0.3 * l)
        lam = (jnp.exp(jnp.sum(lambda_q1[l].astype(jnp.float32) * lambda_k1[l].astype(jnp.float32)))
               - jnp.exp(jnp.sum(lambda_q2[l].astype(jnp.float32) * lambda_k2[l].astype(jnp.float32)))
               + lam_init)
        o_diff = diff_attention(dq, dk, dv, lam).astype(h.dtype)
        o_diff = rmsnorm(o_diff, subln_w[l], SUBLN_EPS) * (1.0 - lam_init)
        o_diff = o_diff.reshape(b, s, DIFF_WIDTH) * jax.nn.silu(dz)

        mixed = (jax.nn.sigmoid(g_ret) * (o_ret @ w_ret_up[l])
                 + jax.nn.sigmoid(g_diff) * (o_diff @ w_diff_up[l]))
        h = h + mixed @ w_out[l]

    return rmsnorm(h, final_norm_w, NORM_EPS)


_drawn_inputs = setup_inputs


def setup_inputs(seed=0):
    import zlib

    import numpy as np

    out = dict(_drawn_inputs(seed))
    spreads = {}
    factors = {'norm_w': 3.48,
     'lambda_q1': 30.988,
     'lambda_q2': 4.15,
     'lambda_k2': 5.648,
     'subln_w': 22.432,
     'final_norm_w': 8.457,
     'lambda_k1': 2.671}
    for name, (base, spread) in spreads.items():
        noise = np.random.default_rng([zlib.crc32(name.encode()), seed]).standard_normal(out[name].shape)
        drawn = base * np.exp(spread * noise) if base else spread * noise
        out[name] = jnp.asarray(drawn.astype(out[name].dtype))
    for name, factor in factors.items():
        out[name] = (out[name] * factor).astype(out[name].dtype)
    return out
```

```python
from contextlib import ExitStack

import numpy as np

import concourse.bass as bass
from concourse import mybir

P = 128
F32 = mybir.dt.float32
F32R = mybir.dt.float32r
ALU = mybir.AluOpType
ACT = mybir.ActivationFunctionType
AX_X = mybir.AxisListType.X

TOKENS, D = 256, 2048
BLOCKS = TOKENS // P
KT = D // P
COLS = 512
KU = 2
UNITS = KT // KU
RING = 4
AHEAD = 3
GROUPS_D = D // COLS

QK = 128
V = 256
HEADS = D // V
QT = COLS // QK

RQ, RK, RV, RZ = 0, 1024, 2048, 4096
DQ, DK, DV, DZ = 6144, 8192, 10240, 12288
G_RET, G_DIFF = 14336, 16384

LAM_INIT = 0.2
NORM_EPS, SUBLN_EPS = 1e-6, 1e-5
MOST_NEGATIVE = -3.4028234663852886e38

RET_ITS, RET_G = 2, 8
UP_ITS, UP_G = 2, 2
DIFF_ITS, DIFF_G = 4, 5
U_RET = 0
U_UP = U_RET + RET_ITS * RET_G * UNITS
U_DIFF = U_UP + UP_ITS * UP_G * UNITS
U_TAIL = U_DIFF + DIFF_ITS * DIFF_G * UNITS
U_OUT = U_TAIL + GROUPS_D * UNITS
U_END = U_OUT + GROUPS_D * UNITS

def ret_uses(it, j):
    return it * 4 + (1 + j)


def up_uses(it, j):
    return it + (9 + j)


def diff_uses_low(it, j):
    return it * 2 + (11 + j)


def diff_uses_high(it, j):
    return it * 4 + (9 + j)


def tail_uses_low(j):
    return 19 + j


def tail_uses_high(j):
    return 25 + j


def diff_fills_67(it, j):
    return it * 3 + (9 + j)


def build(nc, x, norm_w, w_in, w_ret_up, w_diff_up, w_out, lambda_q1, lambda_k1, lambda_q2,
          lambda_k2, subln_w, final_norm_w, rope, decay, causal, out):
    weight = {}
    for name, w in (("in", w_in), ("ret_up", w_ret_up), ("diff_up", w_diff_up), ("out", w_out)):
        weight[name] = w.rearrange("(k p) n -> p k n", p=P)

    with ExitStack() as ctx:
        def sb(name, shape, dt=F32):
            return ctx.enter_context(nc.sbuf_tensor(name, shape, dt))

        def sem(name):
            return ctx.enter_context(nc.semaphore(name))

        raw = sb("raw", [P, RING, KU, COLS])
        w_hi = sb("w_hi", [P, RING, KU, COLS], F32R)
        w_lo = sb("w_lo", [P, RING, KU, COLS], F32R)
        xt_hi = sb("xt_hi", [P, KT, TOKENS], F32R)
        xt_lo = sb("xt_lo", [P, KT, TOKENS], F32R)
        ot_hi = sb("ot_hi", [P, KT, TOKENS], F32R)
        ot_lo = sb("ot_lo", [P, KT, TOKENS], F32R)
        mixed = sb("mixed", [P, BLOCKS, D])
        gate = sb("gate", [P, BLOCKS, D])
        rope_sb = sb("rope_sb", [P, 3, BLOCKS, 192])
        decay_sb = sb("decay_sb", [P, HEADS, TOKENS])
        causal_sb = sb("causal_sb", [P, TOKENS])
        ident = sb("ident", [P, P])
        qT = sb("qT", [P, QT, TOKENS])
        kT = sb("kT", [P, QT, TOKENS])
        v_sb = sb("v_sb", [P, BLOCKS, 2 * COLS])
        zs = sb("zs", [P, BLOCKS, 2 * COLS])
        probs = sb("probs", [P, QT * 3 * P])
        rot_cos = sb("rot_cos", [P, COLS])
        rot_sin = sb("rot_sin", [P, COLS])
        rot = sb("rot", [P, BLOCKS, COLS])
        normed = sb("normed", [P, 2, BLOCKS, V])
        sub08 = sb("sub08", [P, V])
        junk = sb("junk", [P, 2, COLS], mybir.dt.bfloat16)
        rows = sb("rows", [KT, P])
        norm_col = sb("norm_col", [P, KT])
        lam_a = sb("lam_a", [2, P])
        lam_b = sb("lam_b", [2, P])
        lam_dot = sb("lam_dot", [2, 2])
        lam_sign = sb("lam_sign", [2, P])
        neg_lam = sb("neg_lam", [P, 1])
        x_ss = sb("x_ss", [P, 8])
        minus_half = sb("minus_half", [P, 2])
        eps_sb = sb("eps_sb", [P, 4])
        ss = sb("ss", [P, 2, 2])
        ms = sb("ms", [P, 2, 2])
        rstd = sb("rstd", [P, 2, 2])
        row_max = sb("row_max", [P, 2, 4])
        neg_max = sb("neg_max", [P, 2, 4])
        row_sum = sb("row_sum", [P, 2, 4])
        inv_sum = sb("inv_sum", [P, 2, 4])
        h_ss = sb("h_ss", [P, BLOCKS, GROUPS_D])
        h_sum = sb("h_sum", [P, BLOCKS])
        h_ms = sb("h_ms", [P, BLOCKS])
        h_rstd = sb("h_rstd", [P, BLOCKS])
        bank = [ctx.enter_context(nc.psum_tensor(f"bank{b}", [P, COLS], F32)) for b in range(8)]

        x_landed = [sem(f"x_landed{b}") for b in range(BLOCKS)]
        consts_landed = sem("consts_landed")
        tables_landed = sem("tables_landed")
        raw_landed = [sem(f"raw_landed{s}") for s in range(RING)]
        hi_ready = sem("hi_ready")
        units_split = sem("units_split")
        units_done = sem("units_done")
        filled = [sem(f"filled{b}") for b in range(8)]
        drained = [sem(f"drained{b}") for b in range(8)]
        ident_ready = sem("ident_ready")
        pool_consts_ready = sem("pool_consts_ready")
        x_squared = sem("x_squared")
        x_rstd_step = sem("x_rstd_step")
        small_full = sem("small_full")
        x_scaled = sem("x_scaled")
        norm_col_ready = sem("norm_col_ready")
        xt_hi_ready = sem("xt_hi_ready")
        lam_step = sem("lam_step")
        sub_ready = sem("sub_ready")
        lam_sign_step = sem("lam_sign_step")
        neg_lam_ready = sem("neg_lam_ready")
        rot_parts = sem("rot_parts")
        rot_ready = sem("rot_ready")
        z_sigmoid = sem("z_sigmoid")
        z_weighted = sem("z_weighted")
        squares_done = sem("squares_done")
        ms_ready = sem("ms_ready")
        rstd_ready = sem("rstd_ready")
        ot_hi_ready = sem("ot_hi_ready")
        scores_seen = sem("scores_seen")
        neg_max_ready = sem("neg_max_ready")
        exp_done = sem("exp_done")
        comb_step = sem("comb_step")
        attn_ready = sem("attn_ready")
        mixed_ready = sem("mixed_ready")
        mt_hi_ready = sem("mt_hi_ready")
        x_again = sem("x_again")
        h_ready = sem("h_ready")
        h_squared = sem("h_squared")
        h_weighted = sem("h_weighted")
        h_norm_step = sem("h_norm_step")
        y_ready = [sem(f"y_ready{b}") for b in range(BLOCKS)]
        stored = sem("stored")

        def scores_t(m):
            return probs[:, m * 3 * P:(m + 1) * 3 * P]

        def attn_of(a):
            return v_sb[:, a, COLS:COLS + 3 * P]

        def attn_t(a):
            return zs[:, a, COLS:COLS + 3 * P]

        block = ctx.enter_context(nc.Block())

        @block.sync
        def _(sp):
            def load_group(w, n0, col):
                for u in range(UNITS):
                    s = u % RING
                    sp.wait_ge(units_split, n0 + (u + 1))
                    sp.dma_start(raw[:, s, :, :], w[:, u * KU:(u + 1) * KU, bass.ds(col, COLS)]) \
                      .then_inc(raw_landed[s], 16)

            for b in range(BLOCKS):
                sp.dma_start(mixed[:, b, :], x[b * P:(b + 1) * P, :]).then_inc(x_landed[b], 16)
            with sp.Fori(0, RET_ITS) as it:
                n = it * (RET_G * UNITS)
                for pos, (first, step) in enumerate((
                        (RQ, COLS), (RK, COLS), (RZ, 2 * COLS), (RZ + COLS, 2 * COLS), (RV, 2 * COLS),
                        (RV + COLS, 2 * COLS), (G_RET, 2 * COLS), (G_RET + COLS, 2 * COLS))):
                    load_group(weight["in"], n + (U_RET + pos * UNITS), it * step + first)
            with sp.Fori(0, UP_ITS) as it:
                n = it * (UP_G * UNITS)
                for pos in range(UP_G):
                    load_group(weight["ret_up"], n + (U_UP + pos * UNITS), it * (UP_G * COLS) + pos * COLS)
            with sp.Fori(0, DIFF_ITS) as it:
                n = it * (DIFF_G * UNITS)
                for pos, first in enumerate((DQ, DK, DZ, DV, G_DIFF)):
                    load_group(weight["in"], n + (U_DIFF + pos * UNITS), it * COLS + first)
            for j in range(GROUPS_D):
                load_group(weight["diff_up"], U_TAIL + j * UNITS, j * COLS)
            for j in range(GROUPS_D):
                load_group(weight["out"], U_OUT + j * UNITS, j * COLS)
            for half in range(2):
                for b in range(BLOCKS):
                    sp.wait_ge(y_ready[b], half + 1)
                    cols = slice(half * D // 2, (half + 1) * D // 2)
                    sp.dma_start(out[b * P:(b + 1) * P, cols], mixed[:, b, cols]).then_inc(stored, 16)
            sp.wait_ge(stored, 16 * 2 * BLOCKS)

        @block.gpsimd
        def _(pool):
            pool.memset(ident[:], 0.0).then_inc(ident_ready, 1)
            pool.memset(minus_half[:], -0.5).then_inc(pool_consts_ready, 1)
            pool.memset(eps_sb[:, 0:2], NORM_EPS).then_inc(pool_consts_ready, 1)
            pool.memset(eps_sb[:, 2:4], SUBLN_EPS).then_inc(pool_consts_ready, 1)
            pool.wait_ge(pool_consts_ready, 3)
            pool.wait_ge(ident_ready, 1)
            pool.affine_select(out=ident[:], in_=ident[:], compare_op=ALU.not_equal, fill=1.0, base=0,
                               pattern=[[-1, P]], channel_multiplier=1).then_inc(ident_ready, 1)
            for b in range(BLOCKS):
                pool.wait_ge(x_squared, b + 1)
                pool.tensor_scalar(x_ss[:, 2 + b:3 + b], x_ss[:, b:b + 1], 1.0 / D, NORM_EPS,
                                   ALU.mult, ALU.add).then_inc(x_rstd_step, 1)
                pool.wait_ge(x_rstd_step, 2 * b + 1)
                pool.tensor_tensor(x_ss[:, 4 + b:5 + b], x_ss[:, 2 + b:3 + b], minus_half[:, 0:1], ALU.pow) \
                    .then_inc(x_rstd_step, 1)

            def head_rstd(count, m, eps):
                pool.wait_ge(squares_done, count + 1)
                pool.tensor_tensor(ms[:, m % 2, :], ss[:, m % 2, :], eps, ALU.add) \
                    .then_inc(ms_ready, 1)
                pool.wait_ge(ms_ready, count + 1)
                pool.tensor_tensor(rstd[:, m % 2, :], ms[:, m % 2, :], minus_half[:, :], ALU.pow) \
                    .then_inc(rstd_ready, 1)

            with pool.Fori(0, RET_ITS) as it:
                for m in range(4):
                    head_rstd(it * 4 + m, m, eps_sb[:, 0:2])
            with pool.Fori(0, DIFF_ITS) as it:
                pool.wait_ge(sub_ready, 1)
                for b in range(BLOCKS):
                    pool.wait_ge(drained[b], diff_uses_low(it, 0) + 1)
                    z = zs[:, b, 0:COLS].rearrange("p (a e) -> p a e", a=2)
                    pool.tensor_tensor(z, z, sub08[:, :].unsqueeze(1).broadcast_to([P, 2, V]), ALU.mult) \
                        .then_inc(z_weighted, 1)
                for a in range(2):
                    head_rstd(it * 2 + (HEADS + a), a, eps_sb[:, 2:4])
            pool.wait_ge(x_again, 32)
            for j in range(GROUPS_D - 1):
                cols = slice(j * COLS, (j + 1) * COLS)
                for b in range(BLOCKS):
                    pool.wait_ge(h_ready, 2 * j + b + 1)
                    pool.tensor_tensor(mixed[:, b, cols], gate[:, b, cols], zs[:, :, :].rearrange("p b n -> p (b n)")[:, cols],
                                       ALU.mult).then_inc(h_weighted, 1)
            pool.wait_ge(h_norm_step, 2)
            pool.tensor_tensor(h_rstd[:, :], h_ms[:, :], minus_half[:, :], ALU.pow).then_inc(h_norm_step, 1)

        @block.scalar
        def _(act):
            act.dma_start(rows[:, :], norm_w.rearrange("a (k p) -> (a k) p", p=P)).then_inc(consts_landed, 16)
            act.dma_start(lam_a[0:1, :], lambda_q1).then_inc(consts_landed, 16)
            act.dma_start(lam_a[1:2, :], lambda_q2).then_inc(consts_landed, 16)
            act.dma_start(lam_b[0:1, :], lambda_k1).then_inc(consts_landed, 16)
            act.dma_start(lam_b[1:2, :], lambda_k2).then_inc(consts_landed, 16)
            act.dma_start(sub08[:, :], subln_w.broadcast_to([P, V])).then_inc(tables_landed, 16)
            act.dma_start(rope_sb[:], rope.rearrange("s (b p) c -> p s b c", p=P)).then_inc(tables_landed, 16)
            act.dma_start(causal_sb[:], causal).then_inc(tables_landed, 16)
            act.dma_start(decay_sb[:], decay).then_inc(tables_landed, 16)
            act.wait_ge(lam_step, 1)
            act.activation(lam_dot[:, 1:2], lam_dot[:, 0:1], ACT.Exp).then_inc(lam_step, 1)

            def split_hi(n, u):
                s = u % RING
                act.wait_ge(units_done, n + 1)
                act.wait_ge(raw_landed[s], (n - s) * 4 + 16)
                act.activation(w_hi[:, s, :, :], raw[:, s, :, :], ACT.Copy).then_inc(hi_ready, 1)

            def group_done(n_last):
                act.wait_ge(units_done, n_last + (RING + 1))

            def read_qk(dst, b, fills):
                act.wait_ge(filled[4 + b], fills + 1)
                act.activation(dst[:, :, b * P:(b + 1) * P],
                               bank[4 + b][:, :].rearrange("p (m t) -> p m t", m=QT), ACT.Copy) \
                   .then_inc(drained[4 + b], 1)

            def sigmoid_z(n_last, banks, half):
                group_done(n_last)
                for b in range(BLOCKS):
                    act.activation(zs[:, b, half * COLS:(half + 1) * COLS], bank[banks + b][:, :], ACT.Sigmoid) \
                       .then_inc(z_sigmoid, 1)

            def read_v(n_last, banks, half):
                group_done(n_last)
                for b in range(BLOCKS):
                    act.activation(v_sb[:, b, half * COLS:(half + 1) * COLS], bank[banks + b][:, :], ACT.Copy) \
                       .then_inc(drained[banks + b], 1)

            def sigmoid_gate(n_last, banks, dst, col):
                group_done(n_last)
                for b in range(BLOCKS):
                    act.activation(dst[:, b, bass.ds(col, COLS)], bank[banks + b][:, :], ACT.Sigmoid) \
                       .then_inc(drained[banks + b], 1)

            def squares(m, fills):
                act.wait_ge(filled[6 + m % 2], fills + 1)
                for b in range(BLOCKS):
                    last = act.activation(junk[:, m % 2, b * V:(b + 1) * V], bank[6 + m % 2][:, b * V:(b + 1) * V], ACT.Square,
                                          scale=V ** -0.5, accum_out=ss[:, m % 2, b:b + 1])
                last.then_inc(squares_done, 1)

            def read_ot_hi(m, head, fills):
                act.wait_ge(filled[4 + m % 2], fills + 1)
                act.activation(ot_hi[:, bass.ds(head * 2, 2), :],
                               bank[4 + m % 2][:, :].rearrange("p (k t) -> p k t", k=2), ACT.Copy) \
                   .then_inc(ot_hi_ready, 1)

            for b in range(BLOCKS):
                act.wait_ge(x_landed[b], 16)
                act.activation(gate[:, b, :], mixed[:, b, :], ACT.Square, accum_out=x_ss[:, b:b + 1]) \
                   .then_inc(x_squared, 1)
            for u in range(AHEAD):
                split_hi(u, u)
            act.wait_ge(norm_col_ready, 1)
            for j in range(8):
                act.wait_ge(filled[j], 1)
                for k in (2 * j, 2 * j + 1):
                    last = act.activation(xt_hi[:, k, :], bank[j][:, (k % 2) * TOKENS:(k % 2 + 1) * TOKENS],
                                          ACT.Copy, scale=norm_col[:, k:k + 1])
                last.then_inc(xt_hi_ready, 1)

            with act.Fori(0, RET_ITS) as it:
                n0 = it * (RET_G * UNITS) + U_RET
                for s in range(RET_G * UNITS):
                    split_hi(n0 + (s + AHEAD), (s + AHEAD) % UNITS)
                    if s in (11, 13):
                        read_qk(qT, (s - 11) // 2, ret_uses(it, 0))
                    if s in (19, 21):
                        read_qk(kT, (s - 19) // 2, ret_uses(it, 1))
                    if s == 24:
                        sigmoid_z(n0 + 23, 0, 0)
                    if s == 32:
                        sigmoid_z(n0 + 31, 2, 1)
                    if s == 40:
                        read_v(n0 + 39, 0, 0)
                    if s in (43, 44):
                        squares(s - 43, ret_uses(it, 2))
                    if s in (48, 49):
                        read_ot_hi(s - 48, it * 4 + (s - 48), ret_uses(it, 2))
                    if s == 48:
                        read_v(n0 + 47, 2, 1)
                    if s in (51, 52):
                        squares(s - 49, ret_uses(it, 3))
                    if s in (56, 57):
                        read_ot_hi(s - 54, it * 4 + (s - 54), ret_uses(it, 3))
                    if s == 56:
                        sigmoid_gate(n0 + 55, 0, mixed, it * (2 * COLS))
                sigmoid_gate(n0 + 63, 2, mixed, it * (2 * COLS) + COLS)

            with act.Fori(0, UP_ITS) as it:
                n0 = it * (UP_G * UNITS) + U_UP
                for s in range(UP_G * UNITS):
                    split_hi(n0 + (s + AHEAD), (s + AHEAD) % UNITS)

            with act.Fori(0, DIFF_ITS) as it:
                n0 = it * (DIFF_G * UNITS) + U_DIFF
                for s in range(DIFF_G * UNITS):
                    split_hi(n0 + (s + AHEAD), (s + AHEAD) % UNITS)
                    if s in (11, 13):
                        read_qk(qT, (s - 11) // 2, diff_uses_high(it, 0))
                    if s in (19, 21):
                        read_qk(kT, (s - 19) // 2, diff_uses_high(it, 1))
                    if s in (24, 26):
                        a = (s - 24) // 2
                        act.wait_ge(neg_max_ready, it * 2 + (a + 1))
                        for j, (c0, c1) in enumerate(((0, 256), (256, 512), (512, 640), (640, 768))):
                            p = probs[:, a * 6 * P + c0:a * 6 * P + c1]
                            last = act.activation(p, p, ACT.Exp, bias=neg_max[:, a, j:j + 1],
                                                  accum_out=row_sum[:, a, j:j + 1])
                        last.then_inc(exp_done, 1)
                    if s == 27:
                        sigmoid_z(n0 + 23, 0, 0)
                    if s in (30, 32):
                        a = (s - 30) // 2
                        act.wait_ge(filled[4 + a], diff_uses_high(it, 2) + 1)
                        act.activation(attn_t(a), bank[4 + a][:, 0:3 * P], ACT.Copy).then_inc(drained[4 + a], 1)
                    if s == 32:
                        read_v(n0 + 31, 2, 0)
                    if s in (35, 36):
                        squares(s - 35, diff_fills_67(it, 2))
                    if s == 39:
                        read_ot_hi(0, it * 2, diff_uses_high(it, 3))
                sigmoid_gate(n0 + 39, 0, gate, it * COLS)
                read_ot_hi(1, it * 2 + 1, diff_uses_high(it, 3))

            def read_mt_hi(j, half):
                act.wait_ge(filled[4 + half], tail_uses_high(j) + 1)
                k = 4 * j + 2 * half
                act.activation(xt_hi[:, k:k + 2, :], bank[4 + half][:, :].rearrange("p (k t) -> p k t", k=2),
                               ACT.Copy).then_inc(mt_hi_ready, 1)

            def square_h(j):
                for b in range(BLOCKS):
                    act.wait_ge(h_ready, 2 * j + b + 1)
                    if j or b:
                        act.wait_ge(h_squared, 2 * j + b)
                    act.activation(junk[:, b, :], gate[:, b, j * COLS:(j + 1) * COLS], ACT.Square,
                                   accum_out=h_ss[:, b, j:j + 1]).then_inc(h_squared, 1)

            for s in range(2 * GROUPS_D * UNITS):
                if U_TAIL + s + AHEAD < U_END:
                    split_hi(U_TAIL + s + AHEAD, (s + AHEAD) % UNITS)
                g, u = s // UNITS, s % UNITS
                if 1 <= g <= GROUPS_D and u == 2:
                    read_mt_hi(g - 1, 0)
                    read_mt_hi(g - 1, 1)
                if g == GROUPS_D and u == 5:
                    act.wait_ge(mixed_ready, 2 * GROUPS_D)
                    act.dma_start(gate[:, :, :], x.rearrange("(b p) n -> p b n", p=P)).then_inc(x_again, 16)
                    act.dma_start(zs[:, :, :].rearrange("p b n -> p (b n)"), final_norm_w.rearrange("(a n) -> a n", a=1).broadcast_to([P, D])) \
                       .then_inc(x_again, 16)
                if g > GROUPS_D and u == 1:
                    square_h(g - GROUPS_D - 1)
            square_h(GROUPS_D - 1)
            act.wait_ge(h_norm_step, 3)
            act.wait_ge(h_weighted, 2 * GROUPS_D)
            for half in range(2):
                y = mixed[:, 1, half * D // 2:(half + 1) * D // 2]
                act.activation(y, y, ACT.Copy, scale=h_rstd[:, 1:2]).then_inc(y_ready[1], 1)

        @block.vector
        def _(dve):
            dve.sem_inc(units_split, RING)

            def split_lo(n, u):
                s = u % RING
                dve.wait_ge(hi_ready, n + 1)
                dve.tensor_tensor(w_lo[:, s, :, :], raw[:, s, :, :], w_hi[:, s, :, :].bitcast(F32), ALU.subtract) \
                   .then_inc(units_split, 1)

            def group_done(n_last):
                dve.wait_ge(units_done, n_last + (RING + 1))

            def rotate(kind, r, banks, uses, b, first=False):
                if not first:
                    dve.wait_ge(rot_ready, r)
                src = bank[banks + b]
                cos = rope_sb[:, kind, b, 0:64].unsqueeze(1).broadcast_to([P, 2 * QT, 64])
                sin = rope_sb[:, kind, b, 64:192].rearrange("p (s d) -> p s d", s=2).unsqueeze(1) \
                    .broadcast_to([P, QT, 2, 64])
                dve.tensor_tensor(rot_cos[:, :].rearrange("p (g d) -> p g d", d=64),
                                  src[:, :].rearrange("p (g d) -> p g d", d=64), cos, ALU.mult) \
                   .then_inc(rot_parts, 1)
                dve.tensor_tensor(rot_sin[:, :].rearrange("p (m s d) -> p m s d", s=2, d=64),
                                  src[:, :].rearrange("p (m s d) -> p m s d", s=2, d=64)[:, :, ::-1, :],
                                  sin, ALU.mult).then_inc(drained[banks + b], 1)
                dve.wait_ge(rot_parts, r + 1)
                dve.wait_ge(drained[banks + b], uses + 1)
                dve.tensor_tensor(rot[:, b, :], rot_cos[:, :], rot_sin[:, :], ALU.add).then_inc(rot_ready, 1)

            def gate_z(count, banks, half):
                for b in range(BLOCKS):
                    z = zs[:, b, half * COLS:(half + 1) * COLS]
                    dve.wait_ge(z_sigmoid, count + (b + 1))
                    dve.tensor_tensor(z, z, bank[banks + b][:, :], ALU.mult).then_inc(drained[banks + b], 1)

            def norm_head(m, head, zcol):
                src = bank[6 + m % 2]
                dve.wait_ge(rstd_ready, head + 1)
                for b in range(BLOCKS):
                    last = dve.scalar_tensor_tensor(
                        out=normed[:, m % 2, b, :], in0=src[:, b * V:(b + 1) * V],
                        scalar=rstd[:, m % 2, b:b + 1], in1=zs[:, b, zcol:zcol + V],
                        op0=ALU.mult, op1=ALU.mult)
                last.then_inc(drained[6 + m % 2], 1)

            def read_ot_lo(m, head, count):
                dve.wait_ge(ot_hi_ready, count + 1)
                dve.tensor_tensor(ot_lo[:, bass.ds(head * 2, 2), :],
                                  bank[4 + m % 2][:, :].rearrange("p (k t) -> p k t", k=2),
                                  ot_hi[:, bass.ds(head * 2, 2), :].bitcast(F32), ALU.subtract) \
                   .then_inc(drained[4 + m % 2], 1)

            dve.memset(lam_sign[0:2, :], 1.0).then_inc(lam_sign_step, 1)
            dve.wait_ge(lam_sign_step, 1)
            dve.memset(lam_sign[0:1, :], -1.0).then_inc(lam_sign_step, 1)
            dve.wait_ge(consts_landed, 16 * 5)
            dve.tensor_tensor_reduce(out=rot_cos[0:2, 0:P], in0=lam_a[:, :], in1=lam_b[:, :], scale=1.0,
                                     scalar=0.0, op0=ALU.mult, op1=ALU.add, accum_out=lam_dot[:, 0:1]) \
               .then_inc(lam_step, 1)
            dve.wait_ge(small_full, 1)
            dve.tensor_copy(norm_col[:, :], bank[7][:, 0:KT]).then_inc(norm_col_ready, 1)
            dve.tensor_scalar(neg_lam[:, :], bank[7][:, KT:KT + 1], -LAM_INIT, None, ALU.add) \
               .then_inc(neg_lam_ready, 1)
            for b in range(BLOCKS):
                dve.wait_ge(x_rstd_step, 2 * b + 2)
                dve.tensor_scalar(mixed[:, b, :], mixed[:, b, :], x_ss[:, 4 + b:5 + b], None, ALU.mult) \
                   .then_inc(x_scaled, 1)
            for u in range(AHEAD):
                split_lo(u, u)
            for j in range(8):
                dve.wait_ge(xt_hi_ready, j + 1)
                for k in (2 * j, 2 * j + 1):
                    last = dve.scalar_tensor_tensor(
                        out=xt_lo[:, k, :], in0=bank[j][:, (k % 2) * TOKENS:(k % 2 + 1) * TOKENS],
                        scalar=norm_col[:, k:k + 1], in1=xt_hi[:, k, :].bitcast(F32),
                        op0=ALU.mult, op1=ALU.subtract)
                last.then_inc(drained[j], 1)
            dve.wait_ge(tables_landed, 16 * 4)
            dve.tensor_scalar(sub08[:, :], sub08[:, :], 1.0 - LAM_INIT, None, ALU.mult).then_inc(sub_ready, 1)

            with dve.Fori(0, RET_ITS) as it:
                n0 = it * (RET_G * UNITS) + U_RET
                for s in range(RET_G * UNITS):
                    split_lo(n0 + (s + AHEAD), (s + AHEAD) % UNITS)
                    if s in (8, 9):
                        group_done(n0 + 7)
                        rotate(0, it * 4 + (s - 8), 0, ret_uses(it, 0), s - 8, first=s == 8)
                    if s in (16, 17):
                        group_done(n0 + 15)
                        rotate(0, it * 4 + (s - 14), 2, ret_uses(it, 0), s - 16)
                    if s in (24, 25, 27, 28):
                        m = {24: 0, 25: 1, 27: 2, 28: 3}[s]
                        src = bank[6 + m % 2]
                        dve.wait_ge(filled[6 + m % 2], ret_uses(it, m // 2) + 1)
                        head = decay_sb[:, bass.ds(it * 4 + m, 1), :].rearrange("p a t -> p (a t)")
                        dve.tensor_tensor(scores_t(m)[:, 0:2 * P], src[:, 0:2 * P], head, ALU.mult)
                        dve.tensor_tensor(scores_t(m)[:, 2 * P:3 * P], src[:, 2 * P:3 * P], head[:, 0:P], ALU.mult) \
                           .then_inc(drained[6 + m % 2], 1)
                    if s == 26:
                        gate_z(it * 4, 0, 0)
                    if s == 33:
                        gate_z(it * 4 + 2, 2, 1)
                    if s in (44, 45, 52, 53):
                        m = {44: 0, 45: 1, 52: 2, 53: 3}[s]
                        if s in (44, 52):
                            for b in range(BLOCKS):
                                dve.wait_ge(drained[2 * (m // 2) + b], ret_uses(it, 1) + 1)
                        norm_head(m, it * 4 + m, m * V)
                    if s in (49, 50, 57, 58):
                        m = {49: 0, 50: 1, 57: 2, 58: 3}[s]
                        read_ot_lo(m, it * 4 + m, it * 4 + m)

            def merge_ret(n_last, banks, col):
                group_done(n_last)
                for b in range(BLOCKS):
                    part = mixed[:, b, bass.ds(col, COLS)]
                    dve.tensor_tensor(part, part, bank[banks + b][:, :], ALU.mult).then_inc(drained[banks + b], 1)

            with dve.Fori(0, UP_ITS) as it:
                n0 = it * (UP_G * UNITS) + U_UP
                for s in range(UP_G * UNITS):
                    split_lo(n0 + (s + AHEAD), (s + AHEAD) % UNITS)
                    if s == UNITS:
                        merge_ret(n0 + (UNITS - 1), 0, it * (UP_G * COLS))
                merge_ret(n0 + (2 * UNITS - 1), 2, it * (UP_G * COLS) + COLS)

            with dve.Fori(0, DIFF_ITS) as it:
                n0 = it * (DIFF_G * UNITS) + U_DIFF
                for s in range(DIFF_G * UNITS):
                    split_lo(n0 + (s + AHEAD), (s + AHEAD) % UNITS)
                    if s in (8, 9):
                        group_done(n0 + 7)
                        rotate(1, it * 4 + (8 + s - 8), 6, diff_uses_high(it, 0), s - 8, first=s == 8)
                    if s in (16, 17):
                        group_done(n0 + 15)
                        rotate(2, it * 4 + (8 + s - 14), 2, diff_uses_low(it, 0), s - 16)
                    if s in (23, 25):
                        a = (s - 23) // 2
                        for src, keys, c0, j0 in ((6, 2 * P, 0, 0), (7, P, 4 * P, 2)):
                            dve.wait_ge(filled[src], diff_fills_67(it, a) + 1)
                            dve.sem_inc(scores_seen, 1)
                            for c in range(2):
                                p0 = a * 6 * P + c0 + c * keys
                                last = dve.tensor_tensor_reduce(
                                    out=probs[:, p0:p0 + keys], in0=bank[src][:, c * keys:(c + 1) * keys],
                                    in1=causal_sb[:, 2 * P - keys:2 * P], scale=1.0, scalar=MOST_NEGATIVE,
                                    op0=ALU.add, op1=ALU.max, accum_out=row_max[:, a, j0 + c:j0 + c + 1])
                            last.then_inc(drained[src], 1)
                        dve.wait_ge(drained[6], diff_uses_high(it, a + 1) + 1)
                        dve.wait_ge(drained[7], diff_uses_high(it, a + 1) + 1)
                        dve.tensor_scalar(neg_max[:, a, :], row_max[:, a, :], -1.0, None, ALU.mult) \
                           .then_inc(neg_max_ready, 1)
                    if s in (26, 28):
                        a = (s - 26) // 2
                        step = it * 6 + 3 * a
                        p = probs[:, a * 6 * P:(a + 1) * 6 * P]
                        dve.wait_ge(exp_done, it * 2 + (a + 1))
                        dve.reciprocal(inv_sum[:, a, :], row_sum[:, a, :]).then_inc(comb_step, 1)
                        dve.wait_ge(comb_step, step + 1)
                        dve.tensor_scalar(inv_sum[:, a, 1::2], inv_sum[:, a, 1::2], neg_lam[:, 0:1], None, ALU.mult) \
                           .then_inc(comb_step, 1)
                        dve.tensor_scalar(attn_of(a)[:, 0:2 * P], p[:, 0:2 * P], inv_sum[:, a, 0:1], None, ALU.mult)
                        dve.tensor_scalar(attn_of(a)[:, 2 * P:3 * P], p[:, 4 * P:5 * P], inv_sum[:, a, 2:3], None,
                                          ALU.mult).then_inc(comb_step, 1)
                        dve.wait_ge(comb_step, step + 3)
                        dve.scalar_tensor_tensor(out=attn_of(a)[:, 0:2 * P], in0=p[:, 2 * P:4 * P],
                                                 scalar=inv_sum[:, a, 1:2], in1=attn_of(a)[:, 0:2 * P],
                                                 op0=ALU.mult, op1=ALU.add)
                        dve.scalar_tensor_tensor(out=attn_of(a)[:, 2 * P:3 * P], in0=p[:, 5 * P:6 * P],
                                                 scalar=inv_sum[:, a, 3:4], in1=attn_of(a)[:, 2 * P:3 * P],
                                                 op0=ALU.mult, op1=ALU.add).then_inc(attn_ready, 1)
                    if s == 29:
                        gate_z(it * 2 + 4 * RET_ITS, 0, 0)
                    if s in (36, 37):
                        if s == 36:
                            dve.wait_ge(z_weighted, it * 2 + 2)
                        norm_head(s - 36, it * 2 + (HEADS + s - 36), (s - 36) * V)
                for a in range(2):
                    read_ot_lo(a, it * 2 + a, it * 2 + (HEADS + a))

            def merge_diff(j):
                group_done(U_TAIL + (j + 1) * UNITS - 1)
                cols = slice(j * COLS, (j + 1) * COLS)
                banks = 2 * (j % 2)
                for b in range(BLOCKS):
                    dve.tensor_tensor(gate[:, b, cols], gate[:, b, cols], bank[banks + b][:, :], ALU.mult) \
                       .then_inc(drained[banks + b], 1)
                for b in range(BLOCKS):
                    dve.wait_ge(drained[banks + b], tail_uses_low(j // 2) + 1)
                    dve.tensor_tensor(mixed[:, b, cols], mixed[:, b, cols], gate[:, b, cols], ALU.add) \
                       .then_inc(mixed_ready, 1)

            def read_mt_lo(j, half):
                dve.wait_ge(mt_hi_ready, 2 * j + half + 1)
                k = 4 * j + 2 * half
                dve.tensor_tensor(xt_lo[:, k:k + 2, :], bank[4 + half][:, :].rearrange("p (k t) -> p k t", k=2),
                                  xt_hi[:, k:k + 2, :].bitcast(F32), ALU.subtract).then_inc(drained[4 + half], 1)

            def add_residual(j):
                group_done(U_OUT + (j + 1) * UNITS - 1)
                cols = slice(j * COLS, (j + 1) * COLS)
                banks = 2 * (j % 2)
                for b in range(BLOCKS):
                    dve.tensor_tensor(gate[:, b, cols], gate[:, b, cols], bank[banks + b][:, :], ALU.add) \
                       .then_inc(h_ready, 1)
                    dve.wait_ge(h_ready, 2 * j + b + 1)
                    dve.sem_inc(drained[banks + b], 1)

            for s in range(2 * GROUPS_D * UNITS):
                if U_TAIL + s + AHEAD < U_END:
                    split_lo(U_TAIL + s + AHEAD, (s + AHEAD) % UNITS)
                g, u = s // UNITS, s % UNITS
                if 1 <= g <= GROUPS_D:
                    if u == 0:
                        merge_diff(g - 1)
                    if u == 2:
                        read_mt_lo(g - 1, 0)
                        read_mt_lo(g - 1, 1)
                if g > GROUPS_D and u == 0:
                    dve.wait_ge(x_again, 32)
                    add_residual(g - GROUPS_D - 1)

            j = GROUPS_D - 1
            add_residual(j)
            cols = slice(j * COLS, (j + 1) * COLS)
            final_w = zs[:, :, :].rearrange("p b n -> p (b n)")
            for b in range(BLOCKS):
                dve.tensor_tensor(mixed[:, b, cols], gate[:, b, cols], final_w[:, cols], ALU.mult) \
                   .then_inc(h_weighted, 1)
            dve.wait_ge(h_squared, 2 * GROUPS_D)
            dve.tensor_reduce(h_sum[:, :], h_ss[:, :, :], AX_X, ALU.add).then_inc(h_norm_step, 1)
            dve.wait_ge(h_norm_step, 1)
            dve.tensor_scalar(h_ms[:, :], h_sum[:, :], 1.0 / D, NORM_EPS, ALU.mult, ALU.add).then_inc(h_norm_step, 1)
            dve.wait_ge(h_norm_step, 3)
            dve.wait_ge(h_weighted, 2 * GROUPS_D)
            for half in range(2):
                y = mixed[:, 0, half * D // 2:(half + 1) * D // 2]
                dve.tensor_scalar(y, y, h_rstd[:, 0:1], None, ALU.mult).then_inc(y_ready[0], 1)

        @block.tensor
        def _(pe):
            pe.sem_inc(units_done, RING)

            def start_group(banks, uses):
                for b in range(BLOCKS):
                    pe.wait_ge(drained[banks + b], uses)

            def unit(n, u, banks, left_hi, left_lo):
                s = u % RING
                pe.wait_ge(units_split, n + (RING + 1))
                for kk in range(KU):
                    k = u * KU + kk
                    first, last = k == 0, k == KT - 1
                    for b in range(BLOCKS):
                        acc = bank[banks + b][:, :]
                        hi, lo = left_hi[:, k, b * P:(b + 1) * P], left_lo[:, k, b * P:(b + 1) * P]
                        pe.matmul(acc, hi, w_hi[:, s, kk, :], start=first, stop=False)
                        pe.matmul(acc, hi, w_lo[:, s, kk, :], start=False, stop=False)
                        mm = pe.matmul(acc, lo, w_hi[:, s, kk, :], start=False, stop=last)
                mm.then_inc(units_done, 1)

            def transpose_qk(b, r, uses):
                pe.wait_ge(rot_ready, r + 1)
                pe.wait_ge(drained[4 + b], uses)
                for m in range(QT):
                    mm = pe.transpose(bank[4 + b][:, m * P:(m + 1) * P], rot[:, b, m * P:(m + 1) * P], ident[:, :])
                mm.then_inc(filled[4 + b], 1)

            def transpose_head(m, normed_uses, uses):
                pe.wait_ge(drained[6 + m % 2], normed_uses)
                pe.wait_ge(drained[4 + m % 2], uses)
                for e in range(2):
                    for b in range(BLOCKS):
                        c = (2 * e + b) * P
                        mm = pe.transpose(bank[4 + m % 2][:, c:c + P], normed[:, m % 2, b, e * P:(e + 1) * P],
                                          ident[:, :])
                mm.then_inc(filled[4 + m % 2], 1)

            def weights_by_v(dst, v_col, q0k0, q1k0, q1k1):
                v0, v1 = v_sb[:, 0, v_col:v_col + V], v_sb[:, 1, v_col:v_col + V]
                pe.matmul(dst[:, 0:V], q0k0, v0, start=True, stop=True)
                pe.matmul(dst[:, V:2 * V], q1k0, v0, start=True, stop=False)
                return pe.matmul(dst[:, V:2 * V], q1k1, v1, start=False, stop=True)

            pe.wait_ge(ident_ready, 2)
            pe.wait_ge(consts_landed, 16 * 5)
            pe.transpose(bank[7][:, 0:KT], rows[:, :], ident[0:KT, 0:KT])
            pe.wait_ge(lam_sign_step, 2)
            pe.wait_ge(lam_step, 2)
            pe.matmul(bank[7][:, KT:KT + 1], lam_sign[:, :], lam_dot[:, 1:2], start=True, stop=True) \
              .then_inc(small_full, 1)
            pe.wait_ge(norm_col_ready, 1)
            pe.wait_ge(neg_lam_ready, 1)
            for b in range(BLOCKS):
                pe.wait_ge(x_scaled, b + 1)
                for k in range(KT):
                    c = (k % 2) * TOKENS + b * P
                    mm = pe.transpose(bank[k // 2][:, c:c + P], mixed[:, b, k * P:(k + 1) * P], ident[:, :])
                    if b == 1 and k % 2 == 1:
                        mm.then_inc(filled[k // 2], 1)

            with pe.Fori(0, RET_ITS) as it:
                n0 = it * (RET_G * UNITS) + U_RET
                for s in range(RET_G * UNITS):
                    g, u = s // UNITS, s % UNITS
                    if u == 0:
                        start_group(2 * (g % 2), ret_uses(it, g // 2))
                    if g == 0:
                        pe.wait_ge(drained[u], 1)
                    unit(n0 + s, u, 2 * (g % 2), xt_hi, xt_lo)
                    if s in (10, 12):
                        transpose_qk((s - 10) // 2, it * 4 + (s - 10) // 2, ret_uses(it, 0))
                    if s in (18, 20):
                        transpose_qk((s - 18) // 2, it * 4 + (2 + (s - 18) // 2), ret_uses(it, 1))
                    if s in (23, 24, 26, 27):
                        m = {23: 0, 24: 1, 26: 2, 27: 3}[s]
                        for b in range(BLOCKS):
                            pe.wait_ge(drained[4 + b], ret_uses(it, 2))
                        pe.wait_ge(drained[6 + m % 2], ret_uses(it, m // 2))
                        dst = bank[6 + m % 2]
                        pe.matmul(dst[:, 0:2 * P], kT[:, m, 0:P], qT[:, m, :], start=True, stop=True)
                        pe.matmul(dst[:, 2 * P:3 * P], kT[:, m, P:2 * P], qT[:, m, P:2 * P], start=True, stop=True) \
                          .then_inc(filled[6 + m % 2], 1)
                    if s in (42, 43, 50, 51):
                        m = {42: 0, 43: 1, 50: 2, 51: 3}[s]
                        for b in range(BLOCKS):
                            pe.wait_ge(drained[2 * (m // 2) + b], ret_uses(it, 3))
                        pe.wait_ge(drained[6 + m % 2], ret_uses(it, 2 + m // 2))
                        st = scores_t(m)
                        weights_by_v(bank[6 + m % 2], m * V, st[:, 0:P], st[:, P:2 * P], st[:, 2 * P:3 * P]) \
                            .then_inc(filled[6 + m % 2], 1)
                    if s in (46, 47, 54, 55):
                        m = {46: 0, 47: 1, 54: 2, 55: 3}[s]
                        transpose_head(m, ret_uses(it, 3 + m // 2), ret_uses(it, 2 + m // 2))

            for b in range(BLOCKS):
                pe.wait_ge(drained[4 + b], ret_uses(RET_ITS, 0))
            with pe.Fori(0, UP_ITS) as it:
                n0 = it * (UP_G * UNITS) + U_UP
                for s in range(UP_G * UNITS):
                    g, u = s // UNITS, s % UNITS
                    if u == 0:
                        start_group(2 * g, up_uses(it, 0))
                    unit(n0 + s, u, 2 * g, ot_hi, ot_lo)

            with pe.Fori(0, DIFF_ITS) as it:
                n0 = it * (DIFF_G * UNITS) + U_DIFF
                for s in range(DIFF_G * UNITS):
                    g, u = s // UNITS, s % UNITS
                    banks = (6, 2, 0, 2, 0)[g]
                    if u == 0:
                        start_group(banks, diff_uses_high(it, 0) if g == 0 else diff_uses_low(it, (g - 1) // 2))
                    unit(n0 + s, u, banks, xt_hi, xt_lo)
                    if s in (10, 12):
                        transpose_qk((s - 10) // 2, it * 4 + (8 + (s - 10) // 2), diff_uses_high(it, 0))
                    if s in (18, 20):
                        transpose_qk((s - 18) // 2, it * 4 + (10 + (s - 18) // 2), diff_uses_high(it, 1))
                    if s in (22, 24):
                        a = (s - 22) // 2
                        for b in range(BLOCKS):
                            pe.wait_ge(drained[4 + b], diff_uses_high(it, 2))
                            pe.wait_ge(drained[6 + b], diff_uses_high(it, 1 + a))
                        for c in range(2):
                            mm = pe.matmul(bank[6][:, c * 2 * P:(c + 1) * 2 * P], qT[:, 2 * a + c, P:2 * P],
                                           kT[:, 2 * a + c, :], start=True, stop=True)
                        mm.then_inc(filled[6], 1)
                        for c in range(2):
                            mm = pe.matmul(bank[7][:, c * P:(c + 1) * P], qT[:, 2 * a + c, 0:P],
                                           kT[:, 2 * a + c, 0:P], start=True, stop=True)
                        mm.then_inc(filled[7], 1)
                    if s in (28, 30):
                        a = (s - 28) // 2
                        pe.wait_ge(attn_ready, it * 2 + (a + 1))
                        pe.wait_ge(drained[4 + a], diff_uses_high(it, 2))
                        for i in range(3):
                            mm = pe.transpose(bank[4 + a][:, i * P:(i + 1) * P], attn_of(a)[:, i * P:(i + 1) * P],
                                              ident[:, :])
                        mm.then_inc(filled[4 + a], 1)
                    if s in (34, 35):
                        a = s - 34
                        for b in range(BLOCKS):
                            pe.wait_ge(drained[2 + b], diff_uses_low(it, 2))
                        pe.wait_ge(drained[4 + a], diff_uses_high(it, 3))
                        pe.wait_ge(drained[6 + a], diff_uses_high(it, 3))
                        at = attn_t(a)
                        weights_by_v(bank[6 + a], a * V, at[:, 2 * P:3 * P], at[:, 0:P], at[:, P:2 * P]) \
                            .then_inc(filled[6 + a], 1)
                    if s in (38, 39):
                        a = s - 38
                        transpose_head(a, diff_uses_high(it, 4), diff_uses_high(it, 3))

            for s in range(2 * GROUPS_D * UNITS):
                g, u = s // UNITS, s % UNITS
                banks = 2 * (g % 2)
                if u == 0:
                    start_group(banks, tail_uses_low(g // 2))
                if g == 0 and u == 6:
                    for b in range(BLOCKS):
                        pe.wait_ge(drained[4 + b], tail_uses_high(0))
                if g == GROUPS_D and u in (0, 6):
                    for b in range(BLOCKS):
                        pe.wait_ge(drained[4 + b], tail_uses_high(3 + u // 6))
                if g < GROUPS_D:
                    unit(U_TAIL + s, u, banks, ot_hi, ot_lo)
                else:
                    unit(U_TAIL + s, u, banks, xt_hi, xt_lo)
                if 1 <= g <= GROUPS_D and u == 1:
                    j = g - 1
                    for half in range(2):
                        pe.wait_ge(mixed_ready, 2 * j + 2)
                        pe.wait_ge(drained[4 + half], tail_uses_high(j))
                        for kk in range(2):
                            for b in range(BLOCKS):
                                c, k = (2 * kk + b) * P, j * COLS + (2 * half + kk) * P
                                mm = pe.transpose(bank[4 + half][:, c:c + P], mixed[:, b, k:k + P], ident[:, :])
                        mm.then_inc(filled[4 + half], 1)


def shape_constants():
    f = np.float32
    pos = np.arange(TOKENS, dtype=f)
    half = QK // 2
    inv_ret = np.exp(f(-np.log(10000.0)) * np.linspace(0.0, 1.0, half, dtype=f)).astype(f)
    inv_rope = (f(10000.0) ** (-np.arange(0, QK, 2, dtype=f) / f(QK))).astype(f)
    rope = np.empty((3, TOKENS, 3 * half), f)
    for i, (inv, scale) in enumerate(((inv_ret, 1.0), (inv_rope, QK ** -0.5), (inv_rope, 1.0))):
        angle = (pos[:, None] * inv[None, :]).astype(f).astype(np.float64)
        rope[i] = np.concatenate([np.cos(angle), -np.sin(angle), np.sin(angle)], axis=1) * scale
    log_gamma = np.log1p(-np.exp2(-5.0 - np.arange(HEADS)))
    rel = np.arange(TOKENS)[None, :] - np.arange(P)[:, None]
    decay = np.where(rel[:, None, :] >= 0, np.exp(log_gamma[None, :, None] * np.maximum(rel, 0)[:, None, :]), 0.0)
    decay = (decay * QK ** -0.5).astype(f)
    causal = np.zeros((P, TOKENS), f)
    causal[:, P:] = np.where(np.arange(P)[None, :] <= np.arange(P)[:, None], 0.0, MOST_NEGATIVE)
    return {"rope": rope, "decay": decay, "causal": causal}


_INS = ["x", "norm_w", "w_in", "w_ret_up", "w_diff_up", "w_out", "lambda_q1", "lambda_k1", "lambda_q2",
        "lambda_k2", "subln_w", "final_norm_w"]


def kernel(**inputs):
    import concourse.bacc as bacc
    from concourse.bass_utils import run_bass_kernel_spmd

    nc = bacc.Bacc("TRN2", target_bir_lowering=False, num_devices=1)
    arrays = {}
    for name in _INS:
        a = np.ascontiguousarray(inputs[name])
        if name in ("x", "w_in", "w_ret_up", "w_diff_up", "w_out"):
            a = a.reshape(a.shape[1:])
        arrays[name] = a
    arrays.update(shape_constants())
    args = [nc.dram_tensor(f"{n}_dram", a.shape, mybir.dt.from_np(a.dtype), kind="ExternalInput").ap()
            for n, a in arrays.items()]
    out = nc.dram_tensor("out_dram", (TOKENS, D), F32, kind="ExternalOutput").ap()
    build(nc, *args, out)
    result = run_bass_kernel_spmd(nc, [{f"{n}_dram": a for n, a in arrays.items()}], core_ids=[0])
    return result.results[0]["out_dram"].reshape(1, TOKENS, D)
```

```python
from contextlib import ExitStack

import numpy as np

import concourse.bass as bass
from concourse import mybir

P = 128
F32 = mybir.dt.float32
F32R = mybir.dt.float32r
ALU = mybir.AluOpType
ACT = mybir.ActivationFunctionType
AX_X = mybir.AxisListType.X

TOKENS, D = 256, 2048
BLOCKS = TOKENS // P
KT = D // P
COLS = 512
KU = 2
UNITS = KT // KU
RING = 4
AHEAD = 3
GROUPS_D = D // COLS

QK = 128
V = 256
HEADS = D // V
QT = COLS // QK

RQ, RK, RV, RZ = 0, 1024, 2048, 4096
DQ, DK, DV, DZ = 6144, 8192, 10240, 12288
G_RET, G_DIFF = 14336, 16384

LAM_INIT = 0.2
NORM_EPS, SUBLN_EPS = 1e-6, 1e-5
MOST_NEGATIVE = -3.4028234663852886e38

RET_ITS, RET_G = 2, 8
UP_ITS, UP_G = 2, 2
DIFF_ITS, DIFF_G = 4, 5
U_RET = 0
U_UP = U_RET + RET_ITS * RET_G * UNITS
U_DIFF = U_UP + UP_ITS * UP_G * UNITS
U_TAIL = U_DIFF + DIFF_ITS * DIFF_G * UNITS
U_OUT = U_TAIL + GROUPS_D * UNITS
U_END = U_OUT + GROUPS_D * UNITS

HALVINGS = D.bit_length() - 1
X_NORM_STEPS = GROUPS_D + HALVINGS + 2

def ret_uses(it, j):
    return it * 4 + (1 + j)


def up_uses(it, j):
    return it + (9 + j)


def diff_uses_low(it, j):
    return it * 2 + (11 + j)


def diff_uses_high(it, j):
    return it * 4 + (9 + j)


def tail_uses_low(j):
    return 19 + j


def tail_banks(g):
    return 2 - 2 * (g % 2)


def tail_uses_high(j):
    return 25 + j


def diff_fills_67(it, j):
    return it * 3 + (9 + j)


def build(nc, x, norm_w, w_in, w_ret_up, w_diff_up, w_out, lambda_q1, lambda_k1, lambda_q2,
          lambda_k2, subln_w, final_norm_w, rope, decay, causal, out):
    weight = {}
    for name, w in (("in", w_in), ("ret_up", w_ret_up), ("diff_up", w_diff_up), ("out", w_out)):
        weight[name] = w.rearrange("(k p) n -> p k n", p=P)

    with ExitStack() as ctx:
        def sb(name, shape, dt=F32):
            return ctx.enter_context(nc.sbuf_tensor(name, shape, dt))

        def sem(name):
            return ctx.enter_context(nc.semaphore(name))

        raw = sb("raw", [P, RING, KU, COLS])
        w_hi = sb("w_hi", [P, RING, KU, COLS], F32R)
        w_lo = sb("w_lo", [P, RING, KU, COLS], F32R)
        xt_hi = sb("xt_hi", [P, KT, TOKENS], F32R)
        xt_lo = sb("xt_lo", [P, KT, TOKENS], F32R)
        ot_hi = sb("ot_hi", [P, KT, TOKENS], F32R)
        ot_lo = sb("ot_lo", [P, KT, TOKENS], F32R)
        mixed = sb("mixed", [P, BLOCKS, D])
        gate = sb("gate", [P, BLOCKS, D])
        rope_sb = sb("rope_sb", [P, 3, BLOCKS, 192])
        decay_sb = sb("decay_sb", [P, HEADS, TOKENS])
        causal_sb = sb("causal_sb", [P, TOKENS])
        ident = sb("ident", [P, P])
        qT = sb("qT", [P, QT, TOKENS])
        kT = sb("kT", [P, QT, TOKENS])
        v_sb = sb("v_sb", [P, BLOCKS, 2 * COLS])
        zs = sb("zs", [P, BLOCKS, 2 * COLS])
        probs = sb("probs", [P, QT * 3 * P])
        rot_cos = sb("rot_cos", [P, COLS])
        rot_sin = sb("rot_sin", [P, COLS])
        rot = sb("rot", [P, BLOCKS, COLS])
        normed = sb("normed", [P, 2, BLOCKS, V])
        sub08 = sb("sub08", [P, V])
        junk = sb("junk", [P, 2, COLS], mybir.dt.bfloat16)
        rows = sb("rows", [KT, P])
        norm_col = sb("norm_col", [P, KT])
        lam_a = sb("lam_a", [2, P])
        lam_b = sb("lam_b", [2, P])
        lam_junk = sb("lam_junk", [2, P])
        lam_dot = sb("lam_dot", [2, 2])
        lam_sign = sb("lam_sign", [2, P])
        neg_lam = sb("neg_lam", [P, 1])
        x_sum = sb("x_sum", [P, BLOCKS])
        x_rstd = sb("x_rstd", [P, BLOCKS])
        minus_half = sb("minus_half", [P, 2])
        eps_sb = sb("eps_sb", [P, 4])
        warm = sb("warm", [P, 2])
        ss = sb("ss", [P, 2, 2])
        ms = sb("ms", [P, 2, 2])
        rstd = sb("rstd", [P, 2, 2])
        row_max = sb("row_max", [P, 2, 4])
        neg_max = sb("neg_max", [P, 2, 4])
        row_sum = sb("row_sum", [P, 2, 4])
        inv_sum = sb("inv_sum", [P, 2, 4])
        h_ss = sb("h_ss", [P, BLOCKS, GROUPS_D])
        h_sum = sb("h_sum", [P, BLOCKS])
        h_ms = sb("h_ms", [P, BLOCKS])
        h_rstd = sb("h_rstd", [P, BLOCKS])
        bank = [ctx.enter_context(nc.psum_tensor(f"bank{b}", [P, COLS], F32)) for b in range(8)]

        x_landed = [sem(f"x_landed{c}") for c in range(GROUPS_D)]
        norm_w_landed = sem("norm_w_landed")
        lambda_landed = sem("lambda_landed")
        tables_landed = sem("tables_landed")
        raw_landed = [sem(f"raw_landed{s}") for s in range(RING)]
        hi_ready = sem("hi_ready")
        units_split = sem("units_split")
        units_done = sem("units_done")
        filled = [sem(f"filled{b}") for b in range(8)]
        drained = [sem(f"drained{b}") for b in range(8)]
        ident_ready = sem("ident_ready")
        pool_consts_ready = sem("pool_consts_ready")
        x_norm_step = sem("x_norm_step")
        rope_ready = sem("rope_ready")
        norm_col_full = sem("norm_col_full")
        lam_full = sem("lam_full")
        norm_col_ready = sem("norm_col_ready")
        xt_hi_ready = sem("xt_hi_ready")
        lam_step = sem("lam_step")
        sub_ready = sem("sub_ready")
        lam_sign_step = sem("lam_sign_step")
        neg_lam_ready = sem("neg_lam_ready")
        rot_parts = sem("rot_parts")
        rot_ready = sem("rot_ready")
        z_sigmoid = sem("z_sigmoid")
        z_weighted = sem("z_weighted")
        squares_done = sem("squares_done")
        ms_ready = sem("ms_ready")
        rstd_ready = sem("rstd_ready")
        ot_hi_ready = sem("ot_hi_ready")
        scores_seen = sem("scores_seen")
        neg_max_ready = sem("neg_max_ready")
        exp_done = sem("exp_done")
        comb_step = sem("comb_step")
        attn_ready = sem("attn_ready")
        mixed_ready = sem("mixed_ready")
        mt_hi_ready = sem("mt_hi_ready")
        x_again = sem("x_again")
        h_ready = sem("h_ready")
        h_squared = sem("h_squared")
        h_weighted = sem("h_weighted")
        h_norm_step = sem("h_norm_step")
        y_even = sem("y_even")
        y_odd = sem("y_odd")
        stored = sem("stored")

        def scores_t(m):
            return probs[:, m * 3 * P:(m + 1) * 3 * P]

        def attn_of(a):
            return v_sb[:, a, COLS:COLS + 3 * P]

        def attn_t(a):
            return zs[:, a, COLS:COLS + 3 * P]

        def load_x(eng, c):
            cols = slice(c * COLS, (c + 1) * COLS)
            eng.dma_start(mixed[:, :, cols], x[:, cols].rearrange("(b p) n -> p b n", p=P)) \
               .then_inc(x_landed[c], 16)

        block = ctx.enter_context(nc.Block())

        @block.sync
        def _(sp):
            def load_group(w, n0, col):
                for u in range(UNITS):
                    s = u % RING
                    sp.wait_ge(units_split, n0 + (u + 1))
                    sp.dma_start(raw[:, s, :, :], w[:, u * KU:(u + 1) * KU, bass.ds(col, COLS)]) \
                      .then_inc(raw_landed[s], 16)

            sp.dma_start(rows[:, :], norm_w.rearrange("a (k p) -> (a k) p", p=P)).then_inc(norm_w_landed, 16)
            with sp.Fori(0, RET_ITS) as it:
                n = it * (RET_G * UNITS)
                for pos, (first, step) in enumerate((
                        (RQ, COLS), (RK, COLS), (RZ, 2 * COLS), (RZ + COLS, 2 * COLS), (RV, 2 * COLS),
                        (RV + COLS, 2 * COLS), (G_RET, 2 * COLS), (G_RET + COLS, 2 * COLS))):
                    load_group(weight["in"], n + (U_RET + pos * UNITS), it * step + first)
            with sp.Fori(0, UP_ITS) as it:
                n = it * (UP_G * UNITS)
                for pos in range(UP_G):
                    load_group(weight["ret_up"], n + (U_UP + pos * UNITS), it * (UP_G * COLS) + pos * COLS)
            with sp.Fori(0, DIFF_ITS) as it:
                n = it * (DIFF_G * UNITS)
                for pos, first in enumerate((DQ, DK, DZ, DV, G_DIFF)):
                    load_group(weight["in"], n + (U_DIFF + pos * UNITS), it * COLS + first)
            for j in range(GROUPS_D):
                load_group(weight["diff_up"], U_TAIL + j * UNITS, j * COLS)
            for j in range(GROUPS_D):
                load_group(weight["out"], U_OUT + j * UNITS, j * COLS)
            for b in range(BLOCKS):
                for i in range(GROUPS_D // 2):
                    for y_ready in (y_even, y_odd):
                        c = 2 * i + (y_ready is y_odd)
                        sp.wait_ge(y_ready, b * (GROUPS_D // 2) + i + 1)
                        cols = slice(c * COLS, (c + 1) * COLS)
                        sp.dma_start(out[b * P:(b + 1) * P, cols], mixed[:, b, cols]).then_inc(stored, 16)
            sp.wait_ge(stored, 16 * BLOCKS * GROUPS_D)

        @block.gpsimd
        def _(pool):
            pool.memset(ident[:], 0.0).then_inc(ident_ready, 1)
            pool.memset(minus_half[:], -0.5).then_inc(pool_consts_ready, 1)
            pool.memset(eps_sb[:, 0:2], NORM_EPS).then_inc(pool_consts_ready, 1)
            pool.memset(eps_sb[:, 2:4], SUBLN_EPS).then_inc(pool_consts_ready, 1)
            pool.wait_ge(pool_consts_ready, 3)
            pool.wait_ge(ident_ready, 1)
            pool.affine_select(out=ident[:], in_=ident[:], compare_op=ALU.not_equal, fill=1.0, base=0,
                               pattern=[[-1, P]], channel_multiplier=1).then_inc(ident_ready, 1)
            for c in range(GROUPS_D):
                cols = slice(c * COLS, (c + 1) * COLS)
                pool.wait_ge(x_landed[c], 16)
                pool.tensor_tensor(gate[:, :, cols], mixed[:, :, cols], mixed[:, :, cols], ALU.mult) \
                    .then_inc(x_norm_step, 1)
            for i in range(HALVINGS):
                n = D >> (i + 1)
                pool.wait_ge(x_norm_step, GROUPS_D + i)
                pool.tensor_tensor(gate[:, :, 0:n], gate[:, :, 0:n], gate[:, :, n:2 * n], ALU.add) \
                    .then_inc(x_norm_step, 1)
            pool.wait_ge(x_norm_step, X_NORM_STEPS - 2)
            pool.tensor_scalar(x_sum[:, :], gate[:, :, 0], 1.0 / D, NORM_EPS, ALU.mult, ALU.add) \
                .then_inc(x_norm_step, 1)
            pool.wait_ge(x_norm_step, X_NORM_STEPS - 1)
            pool.tensor_tensor(x_rstd[:, :], x_sum[:, :], minus_half[:, :], ALU.pow).then_inc(x_norm_step, 1)
            pool.wait_ge(x_norm_step, X_NORM_STEPS)
            pool.wait_ge(tables_landed, 16 * 4)
            for b in range(BLOCKS):
                pool.tensor_scalar(rope_sb[:, :, b, :], rope_sb[:, :, b, :], x_rstd[:, b:b + 1], 1.0,
                                   ALU.mult, ALU.mult).then_inc(rope_ready, 1)

            def head_rstd(count, m, eps):
                pool.wait_ge(squares_done, count + 1)
                pool.tensor_tensor(ms[:, m % 2, :], ss[:, m % 2, :], eps, ALU.add) \
                    .then_inc(ms_ready, 1)
                pool.wait_ge(ms_ready, count + 1)
                pool.tensor_tensor(rstd[:, m % 2, :], ms[:, m % 2, :], minus_half[:, :], ALU.pow) \
                    .then_inc(rstd_ready, 1)

            with pool.Fori(0, RET_ITS) as it:
                for m in range(4):
                    head_rstd(it * 4 + m, m, eps_sb[:, 0:2])
            with pool.Fori(0, DIFF_ITS) as it:
                pool.wait_ge(sub_ready, 1)
                for b in range(BLOCKS):
                    pool.wait_ge(drained[b], diff_uses_low(it, 0) + 1)
                    z = zs[:, b, 0:COLS].rearrange("p (a e) -> p a e", a=2)
                    pool.tensor_tensor(z, z, sub08[:, :].unsqueeze(1).broadcast_to([P, 2, V]), ALU.mult) \
                        .then_inc(z_weighted, 1)
                for a in range(2):
                    head_rstd(it * 2 + (HEADS + a), a, eps_sb[:, 2:4])
            pool.wait_ge(x_again, 32)
            for j in range(GROUPS_D - 1):
                cols = slice(j * COLS, (j + 1) * COLS)
                for b in range(BLOCKS):
                    pool.wait_ge(h_ready, 2 * j + b + 1)
                    pool.tensor_tensor(mixed[:, b, cols], gate[:, b, cols], zs[:, :, :].rearrange("p b n -> p (b n)")[:, cols],
                                       ALU.mult).then_inc(h_weighted, 1)
            for b in range(BLOCKS):
                pool.wait_ge(h_norm_step, 3 * b + 2)
                pool.tensor_tensor(h_rstd[:, b:b + 1], h_ms[:, b:b + 1], minus_half[:, 0:1], ALU.pow) \
                    .then_inc(h_norm_step, 1)

        @block.scalar
        def _(act):
            for c in range(GROUPS_D):
                load_x(act, c)
            act.wait_ge(pool_consts_ready, 3)
            act.activation(warm[:, :], minus_half[:, :], ACT.Sigmoid)

            def split_hi(n, u):
                s = u % RING
                act.wait_ge(units_done, n + 1)
                act.wait_ge(raw_landed[s], (n - s) * 4 + 16)
                act.activation(w_hi[:, s, :, :], raw[:, s, :, :], ACT.Copy).then_inc(hi_ready, 1)

            def group_done(n_last):
                act.wait_ge(units_done, n_last + (RING + 1))

            def read_qk(dst, b, fills):
                act.wait_ge(filled[4 + b], fills + 1)
                act.activation(dst[:, :, b * P:(b + 1) * P],
                               bank[4 + b][:, :].rearrange("p (m t) -> p m t", m=QT), ACT.Copy) \
                   .then_inc(drained[4 + b], 1)

            def sigmoid_z(n_last, banks, half):
                group_done(n_last)
                for b in range(BLOCKS):
                    act.activation(zs[:, b, half * COLS:(half + 1) * COLS], bank[banks + b][:, :], ACT.Sigmoid,
                                   scale=x_rstd[:, b:b + 1]) \
                       .then_inc(z_sigmoid, 1)

            def read_v(n_last, banks, half):
                group_done(n_last)
                for b in range(BLOCKS):
                    act.activation(v_sb[:, b, half * COLS:(half + 1) * COLS], bank[banks + b][:, :], ACT.Copy,
                                   scale=x_rstd[:, b:b + 1]) \
                       .then_inc(drained[banks + b], 1)

            def sigmoid_gate(n_last, banks, dst, col):
                group_done(n_last)
                for b in range(BLOCKS):
                    act.activation(dst[:, b, bass.ds(col, COLS)], bank[banks + b][:, :], ACT.Sigmoid,
                                   scale=x_rstd[:, b:b + 1]) \
                       .then_inc(drained[banks + b], 1)

            def squares(m, fills):
                act.wait_ge(filled[6 + m % 2], fills + 1)
                for b in range(BLOCKS):
                    last = act.activation(junk[:, m % 2, b * V:(b + 1) * V], bank[6 + m % 2][:, b * V:(b + 1) * V], ACT.Square,
                                          scale=V ** -0.5, accum_out=ss[:, m % 2, b:b + 1])
                last.then_inc(squares_done, 1)

            def read_ot_hi(m, head, fills):
                act.wait_ge(filled[4 + m % 2], fills + 1)
                act.activation(ot_hi[:, bass.ds(head * 2, 2), :],
                               bank[4 + m % 2][:, :].rearrange("p (k t) -> p k t", k=2), ACT.Copy) \
                   .then_inc(ot_hi_ready, 1)

            act.wait_ge(norm_col_ready, 1)
            for j in range(8):
                act.wait_ge(filled[j], 1)
                for k in (2 * j, 2 * j + 1):
                    last = act.activation(xt_hi[:, k, :], bank[j][:, (k % 2) * TOKENS:(k % 2 + 1) * TOKENS],
                                          ACT.Copy, scale=norm_col[:, k:k + 1])
                last.then_inc(xt_hi_ready, 1)
                if j in (0, 2, 4):
                    split_hi(j // 2, j // 2)
            act.dma_start(sub08[:, :], subln_w.broadcast_to([P, V])).then_inc(tables_landed, 16)
            act.dma_start(rope_sb[:], rope.rearrange("s (b p) c -> p s b c", p=P)).then_inc(tables_landed, 16)
            act.dma_start(causal_sb[:], causal).then_inc(tables_landed, 16)
            act.dma_start(decay_sb[:], decay).then_inc(tables_landed, 16)
            act.dma_start(lam_a[0:1, :], lambda_q1).then_inc(lambda_landed, 16)
            act.dma_start(lam_a[1:2, :], lambda_q2).then_inc(lambda_landed, 16)
            act.dma_start(lam_b[0:1, :], lambda_k1).then_inc(lambda_landed, 16)
            act.dma_start(lam_b[1:2, :], lambda_k2).then_inc(lambda_landed, 16)
            with act.Fori(0, RET_ITS) as it:
                n0 = it * (RET_G * UNITS) + U_RET
                for s in range(RET_G * UNITS):
                    split_hi(n0 + (s + AHEAD), (s + AHEAD) % UNITS)
                    if s in (11, 13):
                        read_qk(qT, (s - 11) // 2, ret_uses(it, 0))
                    if s in (19, 21):
                        read_qk(kT, (s - 19) // 2, ret_uses(it, 1))
                    if s == 24:
                        act.wait_ge(x_norm_step, X_NORM_STEPS)
                        sigmoid_z(n0 + 23, 0, 0)
                    if s == 32:
                        sigmoid_z(n0 + 31, 2, 1)
                    if s == 40:
                        read_v(n0 + 39, 0, 0)
                    if s in (43, 44):
                        squares(s - 43, ret_uses(it, 2))
                    if s in (48, 49):
                        read_ot_hi(s - 48, it * 4 + (s - 48), ret_uses(it, 2))
                    if s == 48:
                        read_v(n0 + 47, 2, 1)
                    if s in (51, 52):
                        squares(s - 49, ret_uses(it, 3))
                    if s in (56, 57):
                        read_ot_hi(s - 54, it * 4 + (s - 54), ret_uses(it, 3))
                    if s == 56:
                        sigmoid_gate(n0 + 55, 0, mixed, it * (2 * COLS))
                sigmoid_gate(n0 + 63, 2, mixed, it * (2 * COLS) + COLS)

            act.wait_ge(lam_step, 1)
            act.activation(lam_dot[:, 1:2], lam_dot[:, 0:1], ACT.Exp).then_inc(lam_step, 1)

            with act.Fori(0, UP_ITS) as it:
                n0 = it * (UP_G * UNITS) + U_UP
                for s in range(UP_G * UNITS):
                    split_hi(n0 + (s + AHEAD), (s + AHEAD) % UNITS)

            with act.Fori(0, DIFF_ITS) as it:
                n0 = it * (DIFF_G * UNITS) + U_DIFF
                for s in range(DIFF_G * UNITS):
                    split_hi(n0 + (s + AHEAD), (s + AHEAD) % UNITS)
                    if s in (11, 13):
                        read_qk(qT, (s - 11) // 2, diff_uses_high(it, 0))
                    if s in (19, 21):
                        read_qk(kT, (s - 19) // 2, diff_uses_high(it, 1))
                    if s in (24, 26):
                        a = (s - 24) // 2
                        act.wait_ge(neg_max_ready, it * 2 + (a + 1))
                        for j, (c0, c1) in enumerate(((0, 256), (256, 512), (512, 640), (640, 768))):
                            p = probs[:, a * 6 * P + c0:a * 6 * P + c1]
                            last = act.activation(p, p, ACT.Exp, bias=neg_max[:, a, j:j + 1],
                                                  accum_out=row_sum[:, a, j:j + 1])
                        last.then_inc(exp_done, 1)
                    if s == 27:
                        sigmoid_z(n0 + 23, 0, 0)
                    if s in (30, 32):
                        a = (s - 30) // 2
                        act.wait_ge(filled[4 + a], diff_uses_high(it, 2) + 1)
                        act.activation(attn_t(a), bank[4 + a][:, 0:3 * P], ACT.Copy).then_inc(drained[4 + a], 1)
                    if s == 32:
                        read_v(n0 + 31, 2, 0)
                    if s in (35, 36):
                        squares(s - 35, diff_fills_67(it, 2))
                    if s == 39:
                        read_ot_hi(0, it * 2, diff_uses_high(it, 3))
                sigmoid_gate(n0 + 39, 0, gate, it * COLS)
                read_ot_hi(1, it * 2 + 1, diff_uses_high(it, 3))

            def read_mt_hi(j, half):
                act.wait_ge(filled[4 + half], tail_uses_high(j) + 1)
                k = 4 * j + 2 * half
                act.activation(xt_hi[:, k:k + 2, :], bank[4 + half][:, :].rearrange("p (k t) -> p k t", k=2),
                               ACT.Copy).then_inc(mt_hi_ready, 1)

            def square_h(j, b):
                act.wait_ge(h_ready, 2 * j + b + 1)
                if j or b:
                    act.wait_ge(h_squared, 2 * j + b)
                act.activation(junk[:, b, :], gate[:, b, j * COLS:(j + 1) * COLS], ACT.Square,
                               accum_out=h_ss[:, b, j:j + 1]).then_inc(h_squared, 1)

            for s in range(2 * GROUPS_D * UNITS):
                if U_TAIL + s + AHEAD < U_END:
                    split_hi(U_TAIL + s + AHEAD, (s + AHEAD) % UNITS)
                g, u = s // UNITS, s % UNITS
                if 1 <= g <= GROUPS_D and u == 2:
                    read_mt_hi(g - 1, 0)
                    read_mt_hi(g - 1, 1)
                if g == GROUPS_D and u == 5:
                    act.wait_ge(mixed_ready, 2 * GROUPS_D)
                    act.dma_start(gate[:, :, :], x.rearrange("(b p) n -> p b n", p=P)).then_inc(x_again, 16)
                    act.dma_start(zs[:, :, :].rearrange("p b n -> p (b n)"), final_norm_w.rearrange("(a n) -> a n", a=1).broadcast_to([P, D])) \
                       .then_inc(x_again, 16)
                if g > GROUPS_D and u == 1:
                    for b in range(BLOCKS):
                        square_h(g - GROUPS_D - 1, b)
            for b in range(BLOCKS):
                square_h(GROUPS_D - 1, b)
                act.wait_ge(h_weighted, 2 * (GROUPS_D - 1) + b + 1)
                act.wait_ge(h_norm_step, 3 * b + 3)
                for c in (1, 3):
                    y = mixed[:, b, c * COLS:(c + 1) * COLS]
                    act.activation(y, y, ACT.Copy, scale=h_rstd[:, b:b + 1]).then_inc(y_odd, 1)

        @block.vector
        def _(dve):
            dve.sem_inc(units_split, RING)

            def split_lo(n, u):
                s = u % RING
                dve.wait_ge(hi_ready, n + 1)
                dve.tensor_tensor(w_lo[:, s, :, :], raw[:, s, :, :], w_hi[:, s, :, :].bitcast(F32), ALU.subtract) \
                   .then_inc(units_split, 1)

            def group_done(n_last):
                dve.wait_ge(units_done, n_last + (RING + 1))

            def rotate(kind, r, banks, uses, b, first=False):
                if not first:
                    dve.wait_ge(rot_ready, r)
                src = bank[banks + b]
                cos = rope_sb[:, kind, b, 0:64].unsqueeze(1).broadcast_to([P, 2 * QT, 64])
                sin = rope_sb[:, kind, b, 64:192].rearrange("p (s d) -> p s d", s=2).unsqueeze(1) \
                    .broadcast_to([P, QT, 2, 64])
                dve.tensor_tensor(rot_cos[:, :].rearrange("p (g d) -> p g d", d=64),
                                  src[:, :].rearrange("p (g d) -> p g d", d=64), cos, ALU.mult) \
                   .then_inc(rot_parts, 1)
                dve.tensor_tensor(rot_sin[:, :].rearrange("p (m s d) -> p m s d", s=2, d=64),
                                  src[:, :].rearrange("p (m s d) -> p m s d", s=2, d=64)[:, :, ::-1, :],
                                  sin, ALU.mult).then_inc(drained[banks + b], 1)
                dve.wait_ge(rot_parts, r + 1)
                dve.wait_ge(drained[banks + b], uses + 1)
                dve.tensor_tensor(rot[:, b, :], rot_cos[:, :], rot_sin[:, :], ALU.add).then_inc(rot_ready, 1)

            def gate_z(count, banks, half):
                for b in range(BLOCKS):
                    z = zs[:, b, half * COLS:(half + 1) * COLS]
                    dve.wait_ge(z_sigmoid, count + (b + 1))
                    dve.scalar_tensor_tensor(out=z, in0=z, scalar=x_rstd[:, b:b + 1], in1=bank[banks + b][:, :],
                                             op0=ALU.mult, op1=ALU.mult).then_inc(drained[banks + b], 1)

            def norm_head(m, head, zcol):
                src = bank[6 + m % 2]
                dve.wait_ge(rstd_ready, head + 1)
                for b in range(BLOCKS):
                    last = dve.scalar_tensor_tensor(
                        out=normed[:, m % 2, b, :], in0=src[:, b * V:(b + 1) * V],
                        scalar=rstd[:, m % 2, b:b + 1], in1=zs[:, b, zcol:zcol + V],
                        op0=ALU.mult, op1=ALU.mult)
                last.then_inc(drained[6 + m % 2], 1)

            def read_ot_lo(m, head, count):
                dve.wait_ge(ot_hi_ready, count + 1)
                dve.tensor_tensor(ot_lo[:, bass.ds(head * 2, 2), :],
                                  bank[4 + m % 2][:, :].rearrange("p (k t) -> p k t", k=2),
                                  ot_hi[:, bass.ds(head * 2, 2), :].bitcast(F32), ALU.subtract) \
                   .then_inc(drained[4 + m % 2], 1)

            dve.memset(lam_sign[0:2, :], 1.0).then_inc(lam_sign_step, 1)
            dve.wait_ge(lam_sign_step, 1)
            dve.memset(lam_sign[0:1, :], -1.0).then_inc(lam_sign_step, 1)
            dve.wait_ge(norm_col_full, 1)
            dve.tensor_copy(norm_col[:, :], bank[7][:, 0:KT]).then_inc(norm_col_ready, 1)
            for j in range(8):
                dve.wait_ge(xt_hi_ready, j + 1)
                for k in (2 * j, 2 * j + 1):
                    last = dve.scalar_tensor_tensor(
                        out=xt_lo[:, k, :], in0=bank[j][:, (k % 2) * TOKENS:(k % 2 + 1) * TOKENS],
                        scalar=norm_col[:, k:k + 1], in1=xt_hi[:, k, :].bitcast(F32),
                        op0=ALU.mult, op1=ALU.subtract)
                last.then_inc(drained[j], 1)
                if j in (0, 2, 4):
                    split_lo(j // 2, j // 2)
            with dve.Fori(0, RET_ITS) as it:
                n0 = it * (RET_G * UNITS) + U_RET
                for s in range(RET_G * UNITS):
                    split_lo(n0 + (s + AHEAD), (s + AHEAD) % UNITS)
                    if s == 8:
                        dve.wait_ge(rope_ready, BLOCKS)
                    if s in (8, 9):
                        group_done(n0 + 7)
                        rotate(0, it * 4 + (s - 8), 0, ret_uses(it, 0), s - 8, first=s == 8)
                    if s in (16, 17):
                        group_done(n0 + 15)
                        rotate(0, it * 4 + (s - 14), 2, ret_uses(it, 0), s - 16)
                    if s in (24, 25, 27, 28):
                        m = {24: 0, 25: 1, 27: 2, 28: 3}[s]
                        src = bank[6 + m % 2]
                        dve.wait_ge(filled[6 + m % 2], ret_uses(it, m // 2) + 1)
                        head = decay_sb[:, bass.ds(it * 4 + m, 1), :].rearrange("p a t -> p (a t)")
                        dve.tensor_tensor(scores_t(m)[:, 0:2 * P], src[:, 0:2 * P], head, ALU.mult)
                        dve.tensor_tensor(scores_t(m)[:, 2 * P:3 * P], src[:, 2 * P:3 * P], head[:, 0:P], ALU.mult) \
                           .then_inc(drained[6 + m % 2], 1)
                    if s == 26:
                        gate_z(it * 4, 0, 0)
                    if s == 33:
                        gate_z(it * 4 + 2, 2, 1)
                    if s in (44, 45, 52, 53):
                        m = {44: 0, 45: 1, 52: 2, 53: 3}[s]
                        if s in (44, 52):
                            for b in range(BLOCKS):
                                dve.wait_ge(drained[2 * (m // 2) + b], ret_uses(it, 1) + 1)
                        norm_head(m, it * 4 + m, m * V)
                    if s in (49, 50, 57, 58):
                        m = {49: 0, 50: 1, 57: 2, 58: 3}[s]
                        read_ot_lo(m, it * 4 + m, it * 4 + m)

            dve.wait_ge(lambda_landed, 16 * 4)
            dve.tensor_tensor_reduce(out=lam_junk[:, :], in0=lam_a[:, :], in1=lam_b[:, :], scale=1.0,
                                     scalar=0.0, op0=ALU.mult, op1=ALU.add, accum_out=lam_dot[:, 0:1]) \
               .then_inc(lam_step, 1)
            dve.wait_ge(tables_landed, 16 * 4)
            dve.tensor_scalar(sub08[:, :], sub08[:, :], 1.0 - LAM_INIT, None, ALU.mult).then_inc(sub_ready, 1)

            def merge_ret(n_last, banks, col):
                group_done(n_last)
                for b in range(BLOCKS):
                    part = mixed[:, b, bass.ds(col, COLS)]
                    dve.tensor_tensor(part, part, bank[banks + b][:, :], ALU.mult).then_inc(drained[banks + b], 1)

            with dve.Fori(0, UP_ITS) as it:
                n0 = it * (UP_G * UNITS) + U_UP
                for s in range(UP_G * UNITS):
                    split_lo(n0 + (s + AHEAD), (s + AHEAD) % UNITS)
                    if s == UNITS:
                        merge_ret(n0 + (UNITS - 1), 0, it * (UP_G * COLS))
                merge_ret(n0 + (2 * UNITS - 1), 2, it * (UP_G * COLS) + COLS)
            dve.wait_ge(lam_full, 1)
            dve.tensor_scalar(neg_lam[:, :], bank[5][:, 0:1], -LAM_INIT, None, ALU.add).then_inc(neg_lam_ready, 1)

            with dve.Fori(0, DIFF_ITS) as it:
                n0 = it * (DIFF_G * UNITS) + U_DIFF
                for s in range(DIFF_G * UNITS):
                    split_lo(n0 + (s + AHEAD), (s + AHEAD) % UNITS)
                    if s in (8, 9):
                        group_done(n0 + 7)
                        rotate(1, it * 4 + (8 + s - 8), 6, diff_uses_high(it, 0), s - 8, first=s == 8)
                    if s in (16, 17):
                        group_done(n0 + 15)
                        rotate(2, it * 4 + (8 + s - 14), 2, diff_uses_low(it, 0), s - 16)
                    if s in (23, 25):
                        a = (s - 23) // 2
                        for src, keys, c0, j0 in ((6, 2 * P, 0, 0), (7, P, 4 * P, 2)):
                            dve.wait_ge(filled[src], diff_fills_67(it, a) + 1)
                            dve.sem_inc(scores_seen, 1)
                            for c in range(2):
                                p0 = a * 6 * P + c0 + c * keys
                                last = dve.tensor_tensor_reduce(
                                    out=probs[:, p0:p0 + keys], in0=bank[src][:, c * keys:(c + 1) * keys],
                                    in1=causal_sb[:, 2 * P - keys:2 * P], scale=1.0, scalar=MOST_NEGATIVE,
                                    op0=ALU.add, op1=ALU.max, accum_out=row_max[:, a, j0 + c:j0 + c + 1])
                            last.then_inc(drained[src], 1)
                        dve.wait_ge(drained[6], diff_uses_high(it, a + 1) + 1)
                        dve.wait_ge(drained[7], diff_uses_high(it, a + 1) + 1)
                        dve.tensor_scalar(neg_max[:, a, :], row_max[:, a, :], -1.0, None, ALU.mult) \
                           .then_inc(neg_max_ready, 1)
                    if s in (26, 28):
                        a = (s - 26) // 2
                        step = it * 6 + 3 * a
                        p = probs[:, a * 6 * P:(a + 1) * 6 * P]
                        dve.wait_ge(exp_done, it * 2 + (a + 1))
                        dve.reciprocal(inv_sum[:, a, :], row_sum[:, a, :]).then_inc(comb_step, 1)
                        dve.wait_ge(comb_step, step + 1)
                        dve.tensor_scalar(inv_sum[:, a, 1::2], inv_sum[:, a, 1::2], neg_lam[:, 0:1], None, ALU.mult) \
                           .then_inc(comb_step, 1)
                        dve.tensor_scalar(attn_of(a)[:, 0:2 * P], p[:, 0:2 * P], inv_sum[:, a, 0:1], None, ALU.mult)
                        dve.tensor_scalar(attn_of(a)[:, 2 * P:3 * P], p[:, 4 * P:5 * P], inv_sum[:, a, 2:3], None,
                                          ALU.mult).then_inc(comb_step, 1)
                        dve.wait_ge(comb_step, step + 3)
                        dve.scalar_tensor_tensor(out=attn_of(a)[:, 0:2 * P], in0=p[:, 2 * P:4 * P],
                                                 scalar=inv_sum[:, a, 1:2], in1=attn_of(a)[:, 0:2 * P],
                                                 op0=ALU.mult, op1=ALU.add)
                        dve.scalar_tensor_tensor(out=attn_of(a)[:, 2 * P:3 * P], in0=p[:, 5 * P:6 * P],
                                                 scalar=inv_sum[:, a, 3:4], in1=attn_of(a)[:, 2 * P:3 * P],
                                                 op0=ALU.mult, op1=ALU.add).then_inc(attn_ready, 1)
                    if s == 29:
                        gate_z(it * 2 + 4 * RET_ITS, 0, 0)
                    if s in (36, 37):
                        if s == 36:
                            dve.wait_ge(z_weighted, it * 2 + 2)
                        norm_head(s - 36, it * 2 + (HEADS + s - 36), (s - 36) * V)
                for a in range(2):
                    read_ot_lo(a, it * 2 + a, it * 2 + (HEADS + a))

            def merge_diff(j):
                group_done(U_TAIL + (j + 1) * UNITS - 1)
                cols = slice(j * COLS, (j + 1) * COLS)
                banks = tail_banks(j)
                for b in range(BLOCKS):
                    dve.tensor_tensor(gate[:, b, cols], gate[:, b, cols], bank[banks + b][:, :], ALU.mult) \
                       .then_inc(drained[banks + b], 1)
                for b in range(BLOCKS):
                    dve.wait_ge(drained[banks + b], tail_uses_low(j // 2) + 1)
                    dve.tensor_tensor(mixed[:, b, cols], mixed[:, b, cols], gate[:, b, cols], ALU.add) \
                       .then_inc(mixed_ready, 1)

            def read_mt_lo(j, half):
                dve.wait_ge(mt_hi_ready, 2 * j + half + 1)
                k = 4 * j + 2 * half
                dve.tensor_tensor(xt_lo[:, k:k + 2, :], bank[4 + half][:, :].rearrange("p (k t) -> p k t", k=2),
                                  xt_hi[:, k:k + 2, :].bitcast(F32), ALU.subtract).then_inc(drained[4 + half], 1)

            def add_residual(j, b):
                cols = slice(j * COLS, (j + 1) * COLS)
                bk = tail_banks(j) + b
                dve.tensor_tensor(gate[:, b, cols], gate[:, b, cols], bank[bk][:, :], ALU.add).then_inc(h_ready, 1)
                dve.wait_ge(h_ready, 2 * j + b + 1)
                dve.sem_inc(drained[bk], 1)

            for s in range(2 * GROUPS_D * UNITS):
                if U_TAIL + s + AHEAD < U_END:
                    split_lo(U_TAIL + s + AHEAD, (s + AHEAD) % UNITS)
                g, u = s // UNITS, s % UNITS
                if 1 <= g <= GROUPS_D:
                    if u == 0:
                        merge_diff(g - 1)
                    if u == 2:
                        read_mt_lo(g - 1, 0)
                        read_mt_lo(g - 1, 1)
                if g > GROUPS_D and u == 0:
                    dve.wait_ge(x_again, 32)
                    group_done(U_TAIL + g * UNITS - 1)
                    for b in range(BLOCKS):
                        add_residual(g - GROUPS_D - 1, b)

            j = GROUPS_D - 1
            cols = slice(j * COLS, (j + 1) * COLS)
            final_w = zs[:, :, :].rearrange("p b n -> p (b n)")
            for b in range(BLOCKS):
                dve.wait_ge(filled[tail_banks(j) + b], 2)
                add_residual(j, b)
                if b == 0:
                    dve.wait_ge(h_weighted, 2 * j)
                dve.tensor_tensor(mixed[:, b, cols], gate[:, b, cols], final_w[:, cols], ALU.mult) \
                   .then_inc(h_weighted, 1)
                dve.wait_ge(h_squared, 2 * j + b + 1)
                dve.tensor_reduce(h_sum[:, b:b + 1], h_ss[:, b, :], AX_X, ALU.add).then_inc(h_norm_step, 1)
                dve.wait_ge(h_norm_step, 3 * b + 1)
                dve.tensor_scalar(h_ms[:, b:b + 1], h_sum[:, b:b + 1], 1.0 / D, NORM_EPS, ALU.mult, ALU.add) \
                   .then_inc(h_norm_step, 1)
                dve.wait_ge(h_norm_step, 3 * b + 3)
                for c in (0, 2):
                    y = mixed[:, b, c * COLS:(c + 1) * COLS]
                    dve.tensor_scalar(y, y, h_rstd[:, b:b + 1], None, ALU.mult).then_inc(y_even, 1)

        @block.tensor
        def _(pe):
            pe.sem_inc(units_done, RING)

            def start_group(banks, uses):
                for b in range(BLOCKS):
                    pe.wait_ge(drained[banks + b], uses)

            def unit(n, u, banks, left_hi, left_lo):
                pe.wait_ge(units_split, n + (RING + 1))
                for kk in range(KU):
                    for b in range(BLOCKS):
                        mm = three_passes(u, kk, banks + b, b, left_hi, left_lo)
                mm.then_inc(units_done, 1)

            def three_passes(u, kk, bk, b, left_hi, left_lo):
                s, k = u % RING, u * KU + kk
                hi, lo = left_hi[:, k, b * P:(b + 1) * P], left_lo[:, k, b * P:(b + 1) * P]
                pe.matmul(bank[bk][:, :], hi, w_hi[:, s, kk, :], start=k == 0, stop=False)
                pe.matmul(bank[bk][:, :], hi, w_lo[:, s, kk, :], start=False, stop=False)
                return pe.matmul(bank[bk][:, :], lo, w_hi[:, s, kk, :], start=False, stop=k == KT - 1)

            def transpose_qk(b, r, uses):
                pe.wait_ge(rot_ready, r + 1)
                pe.wait_ge(drained[4 + b], uses)
                for m in range(QT):
                    mm = pe.transpose(bank[4 + b][:, m * P:(m + 1) * P], rot[:, b, m * P:(m + 1) * P], ident[:, :])
                mm.then_inc(filled[4 + b], 1)

            def transpose_head(m, normed_uses, uses):
                pe.wait_ge(drained[6 + m % 2], normed_uses)
                pe.wait_ge(drained[4 + m % 2], uses)
                for e in range(2):
                    for b in range(BLOCKS):
                        c = (2 * e + b) * P
                        mm = pe.transpose(bank[4 + m % 2][:, c:c + P], normed[:, m % 2, b, e * P:(e + 1) * P],
                                          ident[:, :])
                mm.then_inc(filled[4 + m % 2], 1)

            def weights_by_v(dst, v_col, q0k0, q1k0, q1k1):
                v0, v1 = v_sb[:, 0, v_col:v_col + V], v_sb[:, 1, v_col:v_col + V]
                pe.matmul(dst[:, 0:V], q0k0, v0, start=True, stop=True)
                pe.matmul(dst[:, V:2 * V], q1k0, v0, start=True, stop=False)
                return pe.matmul(dst[:, V:2 * V], q1k1, v1, start=False, stop=True)

            pe.wait_ge(ident_ready, 2)
            pe.wait_ge(norm_w_landed, 16)
            pe.transpose(bank[7][:, 0:KT], rows[:, :], ident[0:KT, 0:KT]).then_inc(norm_col_full, 1)
            for k in range(KT):
                if k == KT - 2:
                    pe.wait_ge(norm_col_ready, 1)
                if k % (COLS // P) == 0:
                    pe.wait_ge(x_landed[k * P // COLS], 16)
                for b in range(BLOCKS):
                    c = (k % 2) * TOKENS + b * P
                    mm = pe.transpose(bank[k // 2][:, c:c + P], mixed[:, b, k * P:(k + 1) * P], ident[:, :])
                if k % 2 == 1:
                    mm.then_inc(filled[k // 2], 1)

            with pe.Fori(0, RET_ITS) as it:
                n0 = it * (RET_G * UNITS) + U_RET
                for s in range(RET_G * UNITS):
                    g, u = s // UNITS, s % UNITS
                    if u == 0:
                        start_group(2 * (g % 2), ret_uses(it, g // 2))
                    if g == 0:
                        pe.wait_ge(drained[u], 1)
                    unit(n0 + s, u, 2 * (g % 2), xt_hi, xt_lo)
                    if s in (10, 12):
                        transpose_qk((s - 10) // 2, it * 4 + (s - 10) // 2, ret_uses(it, 0))
                    if s in (18, 20):
                        transpose_qk((s - 18) // 2, it * 4 + (2 + (s - 18) // 2), ret_uses(it, 1))
                    if s in (23, 24, 26, 27):
                        m = {23: 0, 24: 1, 26: 2, 27: 3}[s]
                        for b in range(BLOCKS):
                            pe.wait_ge(drained[4 + b], ret_uses(it, 2))
                        pe.wait_ge(drained[6 + m % 2], ret_uses(it, m // 2))
                        dst = bank[6 + m % 2]
                        pe.matmul(dst[:, 0:2 * P], kT[:, m, 0:P], qT[:, m, :], start=True, stop=True)
                        pe.matmul(dst[:, 2 * P:3 * P], kT[:, m, P:2 * P], qT[:, m, P:2 * P], start=True, stop=True) \
                          .then_inc(filled[6 + m % 2], 1)
                    if s in (42, 43, 50, 51):
                        m = {42: 0, 43: 1, 50: 2, 51: 3}[s]
                        for b in range(BLOCKS):
                            pe.wait_ge(drained[2 * (m // 2) + b], ret_uses(it, 3))
                        pe.wait_ge(drained[6 + m % 2], ret_uses(it, 2 + m // 2))
                        st = scores_t(m)
                        weights_by_v(bank[6 + m % 2], m * V, st[:, 0:P], st[:, P:2 * P], st[:, 2 * P:3 * P]) \
                            .then_inc(filled[6 + m % 2], 1)
                    if s in (46, 47, 54, 55):
                        m = {46: 0, 47: 1, 54: 2, 55: 3}[s]
                        transpose_head(m, ret_uses(it, 3 + m // 2), ret_uses(it, 2 + m // 2))

            for b in range(BLOCKS):
                pe.wait_ge(drained[4 + b], ret_uses(RET_ITS, 0))
            with pe.Fori(0, UP_ITS) as it:
                n0 = it * (UP_G * UNITS) + U_UP
                for s in range(UP_G * UNITS):
                    g, u = s // UNITS, s % UNITS
                    if u == 0:
                        start_group(2 * g, up_uses(it, 0))
                    unit(n0 + s, u, 2 * g, ot_hi, ot_lo)

            pe.wait_ge(lam_sign_step, 2)
            pe.wait_ge(lam_step, 2)
            pe.wait_ge(drained[5], ret_uses(RET_ITS, 0))
            pe.matmul(bank[5][:, 0:1], lam_sign[:, :], lam_dot[:, 1:2], start=True, stop=True).then_inc(lam_full, 1)

            with pe.Fori(0, DIFF_ITS) as it:
                n0 = it * (DIFF_G * UNITS) + U_DIFF
                for s in range(DIFF_G * UNITS):
                    g, u = s // UNITS, s % UNITS
                    banks = (6, 2, 0, 2, 0)[g]
                    if u == 0:
                        start_group(banks, diff_uses_high(it, 0) if g == 0 else diff_uses_low(it, (g - 1) // 2))
                    unit(n0 + s, u, banks, xt_hi, xt_lo)
                    if s == 12:
                        pe.wait_ge(neg_lam_ready, 1)
                    if s in (10, 12):
                        transpose_qk((s - 10) // 2, it * 4 + (8 + (s - 10) // 2), diff_uses_high(it, 0))
                    if s in (18, 20):
                        transpose_qk((s - 18) // 2, it * 4 + (10 + (s - 18) // 2), diff_uses_high(it, 1))
                    if s in (22, 24):
                        a = (s - 22) // 2
                        for b in range(BLOCKS):
                            pe.wait_ge(drained[4 + b], diff_uses_high(it, 2))
                            pe.wait_ge(drained[6 + b], diff_uses_high(it, 1 + a))
                        for c in range(2):
                            mm = pe.matmul(bank[6][:, c * 2 * P:(c + 1) * 2 * P], qT[:, 2 * a + c, P:2 * P],
                                           kT[:, 2 * a + c, :], start=True, stop=True)
                        mm.then_inc(filled[6], 1)
                        for c in range(2):
                            mm = pe.matmul(bank[7][:, c * P:(c + 1) * P], qT[:, 2 * a + c, 0:P],
                                           kT[:, 2 * a + c, 0:P], start=True, stop=True)
                        mm.then_inc(filled[7], 1)
                    if s in (28, 30):
                        a = (s - 28) // 2
                        pe.wait_ge(attn_ready, it * 2 + (a + 1))
                        pe.wait_ge(drained[4 + a], diff_uses_high(it, 2))
                        for i in range(3):
                            mm = pe.transpose(bank[4 + a][:, i * P:(i + 1) * P], attn_of(a)[:, i * P:(i + 1) * P],
                                              ident[:, :])
                        mm.then_inc(filled[4 + a], 1)
                    if s in (34, 35):
                        a = s - 34
                        for b in range(BLOCKS):
                            pe.wait_ge(drained[2 + b], diff_uses_low(it, 2))
                        pe.wait_ge(drained[4 + a], diff_uses_high(it, 3))
                        pe.wait_ge(drained[6 + a], diff_uses_high(it, 3))
                        at = attn_t(a)
                        weights_by_v(bank[6 + a], a * V, at[:, 2 * P:3 * P], at[:, 0:P], at[:, P:2 * P]) \
                            .then_inc(filled[6 + a], 1)
                    if s in (38, 39):
                        a = s - 38
                        transpose_head(a, diff_uses_high(it, 4), diff_uses_high(it, 3))

            for s in range(2 * GROUPS_D * UNITS - RING):
                g, u = s // UNITS, s % UNITS
                banks = tail_banks(g)
                if u == 0:
                    start_group(banks, tail_uses_low(g // 2))
                if g == 0 and u == 6:
                    for b in range(BLOCKS):
                        pe.wait_ge(drained[4 + b], tail_uses_high(0))
                if g == GROUPS_D and u in (0, 6):
                    for b in range(BLOCKS):
                        pe.wait_ge(drained[4 + b], tail_uses_high(3 + u // 6))
                if g < GROUPS_D:
                    unit(U_TAIL + s, u, banks, ot_hi, ot_lo)
                else:
                    unit(U_TAIL + s, u, banks, xt_hi, xt_lo)
                if 1 <= g <= GROUPS_D and u == 1:
                    j = g - 1
                    for half in range(2):
                        pe.wait_ge(mixed_ready, 2 * j + 2)
                        pe.wait_ge(drained[4 + half], tail_uses_high(j))
                        for kk in range(2):
                            for b in range(BLOCKS):
                                c, k = (2 * kk + b) * P, j * COLS + (2 * half + kk) * P
                                mm = pe.transpose(bank[4 + half][:, c:c + P], mixed[:, b, k:k + P], ident[:, :])
                        mm.then_inc(filled[4 + half], 1)
            for b in range(BLOCKS):
                for u in range(UNITS - RING, UNITS):
                    if b == 0:
                        pe.wait_ge(units_split, U_END - UNITS + u + (RING + 1))
                    for kk in range(KU):
                        mm = three_passes(u, kk, tail_banks(GROUPS_D - 1) + b, b, xt_hi, xt_lo)
                mm.then_inc(filled[tail_banks(GROUPS_D - 1) + b], 1)


def shape_constants():
    f = np.float32
    pos = np.arange(TOKENS, dtype=f)
    half = QK // 2
    inv_ret = np.exp(f(-np.log(10000.0)) * np.linspace(0.0, 1.0, half, dtype=f)).astype(f)
    inv_rope = (f(10000.0) ** (-np.arange(0, QK, 2, dtype=f) / f(QK))).astype(f)
    rope = np.empty((3, TOKENS, 3 * half), f)
    for i, (inv, scale) in enumerate(((inv_ret, 1.0), (inv_rope, QK ** -0.5), (inv_rope, 1.0))):
        angle = (pos[:, None] * inv[None, :]).astype(f).astype(np.float64)
        rope[i] = np.concatenate([np.cos(angle), -np.sin(angle), np.sin(angle)], axis=1) * scale
    log_gamma = np.log1p(-np.exp2(-5.0 - np.arange(HEADS)))
    rel = np.arange(TOKENS)[None, :] - np.arange(P)[:, None]
    decay = np.where(rel[:, None, :] >= 0, np.exp(log_gamma[None, :, None] * np.maximum(rel, 0)[:, None, :]), 0.0)
    decay = (decay * QK ** -0.5).astype(f)
    causal = np.zeros((P, TOKENS), f)
    causal[:, P:] = np.where(np.arange(P)[None, :] <= np.arange(P)[:, None], 0.0, MOST_NEGATIVE)
    return {"rope": rope, "decay": decay, "causal": causal}


_INS = ["x", "norm_w", "w_in", "w_ret_up", "w_diff_up", "w_out", "lambda_q1", "lambda_k1", "lambda_q2",
        "lambda_k2", "subln_w", "final_norm_w"]


def kernel(**inputs):
    import concourse.bacc as bacc
    from concourse.bass_utils import run_bass_kernel_spmd

    nc = bacc.Bacc("TRN2", target_bir_lowering=False, num_devices=1)
    arrays = {}
    for name in _INS:
        a = np.ascontiguousarray(inputs[name])
        if name in ("x", "w_in", "w_ret_up", "w_diff_up", "w_out"):
            a = a.reshape(a.shape[1:])
        arrays[name] = a
    arrays.update(shape_constants())
    args = [nc.dram_tensor(f"{n}_dram", a.shape, mybir.dt.from_np(a.dtype), kind="ExternalInput").ap()
            for n, a in arrays.items()]
    out = nc.dram_tensor("out_dram", (TOKENS, D), F32, kind="ExternalOutput").ap()
    build(nc, *args, out)
    result = run_bass_kernel_spmd(nc, [{f"{n}_dram": a for n, a in arrays.items()}], core_ids=[0])
    return result.results[0]["out_dram"].reshape(1, TOKENS, D)
```
